# Optimizing a Trainium2 kernel written in Bass

```python
import jax, jax.numpy as jnp
from jax import lax
import numpy as np

D_MODEL = 1024
BATCH = 1
SEQ = 128
DEPTH = 2
DEC_BATCH = 1
DEC_SEQ = 2048
PAST_LEN = 256

GRID_W = 64
HEAD_DIM = 64
N_RWKV = 4
N_NA = 6
N_MLA = 6
D_RWKV = N_RWKV * HEAD_DIM
D_NA = N_NA * HEAD_DIM
MLA_NOPE = 64
MLA_ROPE = 32
MLA_V = 64
D_MLA = N_MLA * MLA_V
D_MIX = D_RWKV + D_NA + D_MLA
MLA_Q_RANK = 256
MLA_KV_RANK = 128
LORA_W = 64
LORA_A = 64
NA_ROWS = 8
NA_COLS = 16
Q_BLOCK = 128
ROPE_BASE = 10000.0
EPS = 1e-6
GN_EPS = 64e-5
NEG_INF = -1e30
MLA_SCALE = (MLA_NOPE + MLA_ROPE) ** -0.5
PROJ_SPLITS = (D_RWKV, D_RWKV, D_RWKV, LORA_W, LORA_A, D_RWKV,
               D_NA, D_NA, D_NA, D_NA,
               MLA_Q_RANK, MLA_KV_RANK, MLA_ROPE, D_MLA)
D_PROJ = sum(PROJ_SPLITS)
SPLIT_POINTS = tuple(int(s) for s in np.cumsum(PROJ_SPLITS)[:-1])

kernel_name = 'hybrid_rwkv7_natten_mla_diffusion_step'

def rms_norm(x, g, eps=EPS):
    xf = x.astype(jnp.float32)
    y = xf * lax.rsqrt(jnp.mean(xf * xf, -1, keepdims=True) + eps)
    return (y * g).astype(x.dtype)

def heads(x, h):
    return x.reshape(x.shape[:-1] + (h, -1))

def centred_conv(x, w):
    xp = jnp.pad(x, ((0, 0), (1, 1), (0, 0)))
    return xp[:, :-2] * w[0] + xp[:, 1:-1] * w[1] + xp[:, 2:] * w[2]

def axial_rope(x):
    T = x.shape[1]
    t = jnp.arange(T)
    n_freq = MLA_ROPE // 4
    inv = jnp.power(ROPE_BASE, -jnp.arange(n_freq, dtype=jnp.float32) / n_freq)
    ang = jnp.concatenate([(t // GRID_W).astype(jnp.float32)[:, None] * inv,
                           (t % GRID_W).astype(jnp.float32)[:, None] * inv], -1)
    cos = jnp.cos(ang)[None, :, None, :]
    sin = jnp.sin(ang)[None, :, None, :]
    x1 = x[..., :MLA_ROPE // 2].astype(jnp.float32)
    x2 = x[..., MLA_ROPE // 2:].astype(jnp.float32)
    return jnp.concatenate([x1 * cos - x2 * sin, x2 * cos + x1 * sin], -1).astype(x.dtype)

def blocked_attention(q, k, v, scale):
    B, T, H, dk = q.shape
    nb = T // Q_BLOCK
    qb = q.reshape(B, nb, Q_BLOCK, H, dk).transpose(1, 0, 2, 3, 4)

    def one(qi):
        s = jnp.einsum('bqhd,bkhd->bhqk', qi, k).astype(jnp.float32) * scale
        p = jax.nn.softmax(s, -1).astype(v.dtype)
        return jnp.einsum('bhqk,bkhd->bqhd', p, v)

    o = lax.map(one, qb)
    return o.transpose(1, 0, 2, 3, 4).reshape(B, T, H, v.shape[-1])

def neighbourhood_attention(q, k, v, k_ctx, v_ctx, rpb):
    B, T, H, dh = q.shape
    rows = T // GRID_W
    kr = min(NA_ROWS, rows)
    qc = np.arange(GRID_W)
    cs = np.clip(qc - NA_COLS // 2, 0, GRID_W - NA_COLS)
    col_mask = (qc[None, :] >= cs[:, None]) & (qc[None, :] < cs[:, None] + NA_COLS)
    dc_idx = np.clip(qc[None, :] - qc[:, None], -(NA_COLS - 1), NA_COLS - 1) + NA_COLS - 1
    rpb_c = rpb[:, :, dc_idx]
    scale = dh ** -0.5
    k_g = k.reshape(B, rows, GRID_W, H, dh)
    v_g = v.reshape(B, rows, GRID_W, H, dh)
    q_rows = q.reshape(B, rows, GRID_W, H, dh).transpose(1, 0, 2, 3, 4)

    def row_block(args):
        r, q_r = args
        rs = jnp.clip(r - kr // 2, 0, rows - kr)
        k_b = lax.dynamic_slice_in_dim(k_g, rs, kr, axis=1)
        v_b = lax.dynamic_slice_in_dim(v_g, rs, kr, axis=1)
        dr_idx = rs + jnp.arange(kr) - r + NA_ROWS - 1
        bias = jnp.take(rpb_c, dr_idx, axis=1).transpose(0, 2, 1, 3)
        s_loc = jnp.einsum('bqhd,bjkhd->bhqjk', q_r, k_b).astype(jnp.float32) * scale + bias.astype(jnp.float32)
        s_loc = jnp.where(col_mask[:, None, :], s_loc, NEG_INF).reshape(B, H, GRID_W, kr * GRID_W)
        s_ctx = jnp.einsum('bqhd,bchd->bhqc', q_r, k_ctx).astype(jnp.float32) * scale
        p = jax.nn.softmax(jnp.concatenate([s_loc, s_ctx], -1), -1).astype(v.dtype)
        p_loc = p[..., :kr * GRID_W].reshape(B, H, GRID_W, kr, GRID_W)
        return (jnp.einsum('bhqjk,bjkhd->bqhd', p_loc, v_b)
                + jnp.einsum('bhqc,bchd->bqhd', p[..., kr * GRID_W:], v_ctx))

    o = lax.map(row_block, (jnp.arange(rows), q_rows))
    return o.transpose(1, 0, 2, 3, 4).reshape(B, T, H * dh)

def both_dirs(x):
    return jnp.stack([x, jnp.flip(x, 1)], 2)

def per_dir(x):
    return jnp.stack([x[:, :, 0], jnp.flip(x[:, :, 1], 1)], 2)

def rwkv_step(S, inp):
    r, w, k, v, kk, a = inp
    sa = jnp.einsum('bdhvk,bdhk->bdhv', S, -kk)
    S = S * w[..., None, :] + sa[..., :, None] * (kk * a)[..., None, :] + v[..., :, None] * k[..., None, :]
    return S, jnp.einsum('bdhvk,bdhk->bdhv', S, r)

def rwkv_mixer(r, k, v, wd, ad, g, s0, l, P):
    B, T, C = r.shape
    f32 = jnp.float32
    w_log = -jax.nn.softplus(-(P['rwkv_w0'][l] + jnp.einsum('btl,dlc->btdc', jnp.tanh(wd), P['rwkv_w_up'][l]))) - 0.5
    decay = jnp.exp(-jnp.exp(w_log.astype(f32)))
    a = jax.nn.sigmoid(P['rwkv_a0'][l] + jnp.einsum('btl,dlc->btdc', ad, P['rwkv_a_up'][l]))
    kk = heads((k * P['rwkv_k_k'][l]).astype(f32), N_RWKV)
    kk = kk / jnp.maximum(jnp.sqrt(jnp.sum(kk * kk, -1, keepdims=True)), 1e-12)
    k_d = k[:, :, None, :] * (1 + (a - 1) * P['rwkv_k_a'][l])
    hd = lambda z: z.reshape(B, T, 2, N_RWKV, HEAD_DIM)
    r_h, v_h = heads(r, N_RWKV), heads(v, N_RWKV)
    k_dh, a_h, w_h = hd(k_d), hd(a), hd(decay)
    seq = tuple(jnp.moveaxis(z.astype(f32), 1, 0) for z in
                (both_dirs(r_h), per_dir(w_h), per_dir(k_dh), both_dirs(v_h), both_dirs(kk), per_dir(a_h)))
    s_fin, ys = lax.scan(rwkv_step, s0.astype(f32), seq)
    ys = jnp.moveaxis(ys, 0, 1)
    o = ys[:, :, 0] + jnp.flip(ys[:, :, 1], 1)
    mu = jnp.mean(o, -1, keepdims=True)
    var = jnp.mean(jnp.square(o - mu), -1, keepdims=True)
    o = ((o - mu) * lax.rsqrt(var + GN_EPS)).reshape(B, T, C) * P['rwkv_ln_w'][l] + P['rwkv_ln_b'][l]
    coef = jnp.sum(jnp.sum(r_h[:, :, None] * k_dh * P['rwkv_r_k'][l], -1, keepdims=True), 2)
    o = o + (coef * v_h).reshape(B, T, C)
    return o.astype(r.dtype) * jax.nn.silu(g), s_fin

def mla_q(cq, l, P, rope):
    q = heads(rms_norm(cq, P['mla_cq_norm'][l]) @ P['mla_w_uq'][l], N_MLA)
    q = rms_norm(q, P['mla_q_norm'][l])
    if rope:
        q = jnp.concatenate([q[..., :MLA_NOPE], axial_rope(q[..., MLA_NOPE:])], -1)
    return q

def mla_kv(ckv_n, krope, l, P, rope):
    B, T, _ = ckv_n.shape
    k_nope = heads(ckv_n @ P['mla_w_uk'][l], N_MLA)
    k_r = jnp.broadcast_to(krope[:, :, None, :], (B, T, N_MLA, MLA_ROPE))
    k = rms_norm(jnp.concatenate([k_nope, k_r], -1), P['mla_k_norm'][l])
    if rope:
        k = jnp.concatenate([k[..., :MLA_NOPE], axial_rope(k[..., MLA_NOPE:])], -1)
    v = heads(ckv_n @ P['mla_w_uv'][l], N_MLA)
    return k, v

def split_proj(x, cond, l, P):
    mod = jax.nn.silu(cond) @ P['w_mod'][l] + P['b_mod'][l]
    shift, scale, gate = jnp.split(mod, 3, -1)
    h = rms_norm(x, P['norm_w'][l]) * (1 + scale) + shift
    return jnp.split(h @ P['w_in'][l], SPLIT_POINTS, -1), gate

def context_layer(x, c_ctx, l, P):
    B, L, _ = x.shape
    (r, k, v, wd, ad, g_r, q_n, k_n, v_n, g_n, cq, ckv, krope, g_m), gate = split_proj(x, c_ctx, l, P)
    r, k, v = jnp.split(centred_conv(jnp.concatenate([r, k, v], -1), P['rwkv_conv'][l]), 3, -1)
    s0 = jnp.zeros((B, 2, N_RWKV, HEAD_DIM, HEAD_DIM), jnp.float32)
    o_r, s_fin = rwkv_mixer(r, k, v, wd, ad, g_r, s0, l, P)
    qn = rms_norm(heads(q_n, N_NA), P['na_q_norm'][l])
    kn = rms_norm(heads(k_n, N_NA), P['na_k_norm'][l])
    vn = heads(v_n, N_NA)
    o_n = blocked_attention(qn, kn, vn, HEAD_DIM ** -0.5).reshape(B, L, D_NA) * jax.nn.silu(g_n)
    ckv_n = rms_norm(ckv, P['mla_ckv_norm'][l])
    qm = mla_q(cq, l, P, False)
    km, vm = mla_kv(ckv_n, krope, l, P, False)
    o_m = blocked_attention(qm, km, vm, MLA_SCALE).reshape(B, L, D_MLA) * jax.nn.silu(g_m)
    y = x + gate * (jnp.concatenate([o_r, o_n, o_m], -1) @ P['w_out'][l])
    return y, (s_fin, kn, vn, ckv_n, krope)

def latent_layer(x, c, s0, k_ctx, v_ctx, ckv_ctx, krope_ctx, l, P):
    B, T, _ = x.shape
    (r, k, v, wd, ad, g_r, q_n, k_n, v_n, g_n, cq, ckv, krope, g_m), gate = split_proj(x, c[:, None, :], l, P)
    r, k, v = jnp.split(centred_conv(jnp.concatenate([r, k, v], -1), P['rwkv_conv'][l]), 3, -1)
    o_r, _ = rwkv_mixer(r, k, v, wd, ad, g_r, s0, l, P)
    qn = rms_norm(heads(q_n, N_NA), P['na_q_norm'][l])
    kn = rms_norm(heads(k_n, N_NA), P['na_k_norm'][l])
    vn = heads(v_n, N_NA)
    o_n = neighbourhood_attention(qn, kn, vn, k_ctx, v_ctx, P['na_rpb'][l]) * jax.nn.silu(g_n)
    ckv_n = rms_norm(ckv, P['mla_ckv_norm'][l])
    qm = mla_q(cq, l, P, True)
    km, vm = mla_kv(ckv_n, krope, l, P, True)
    kc, vc = mla_kv(ckv_ctx, krope_ctx, l, P, False)
    o_m = blocked_attention(qm, jnp.concatenate([kc, km], 1), jnp.concatenate([vc, vm], 1), MLA_SCALE)
    o_m = o_m.reshape(B, T, D_MLA) * jax.nn.silu(g_m)
    return x + gate * (jnp.concatenate([o_r, o_n, o_m], -1) @ P['w_out'][l])

def setup_inputs(seed: int = 0) -> dict:
    key = jax.random.key(seed)
    ks = iter(jax.random.split(key, 48))
    nrm = lambda shape, s=1.0: s * jax.random.normal(next(ks), shape, jnp.float32)
    inp = {}
    inp['x_prompt'] = nrm((BATCH, SEQ, D_MODEL))
    inp['x_sample'] = nrm((DEC_BATCH, DEC_SEQ, D_MODEL))
    inp['state_rwkv'] = nrm((DEC_BATCH, DEPTH, 2, N_RWKV, HEAD_DIM, HEAD_DIM), 0.5)
    inp['cache_na_k'] = nrm((DEC_BATCH, DEPTH, PAST_LEN, N_NA, HEAD_DIM))
    inp['cache_na_v'] = nrm((DEC_BATCH, DEPTH, PAST_LEN, N_NA, HEAD_DIM))
    inp['cache_mla_ckv'] = nrm((DEC_BATCH, DEPTH, PAST_LEN, MLA_KV_RANK))
    inp['cache_mla_krope'] = nrm((DEC_BATCH, DEPTH, PAST_LEN, MLA_ROPE))
    inp['c'] = nrm((DEC_BATCH, D_MODEL))
    inp['c_ctx'] = nrm((D_MODEL,))
    inp['w_mod'] = nrm((DEPTH, D_MODEL, 3 * D_MODEL), 0.5 * D_MODEL ** -0.5)
    inp['b_mod'] = nrm((DEPTH, 3 * D_MODEL), 0.02)
    inp['norm_w'] = 1.0 + nrm((DEPTH, D_MODEL), 0.02)
    inp['w_in'] = nrm((DEPTH, D_MODEL, D_PROJ), D_MODEL ** -0.5)
    inp['w_out'] = nrm((DEPTH, D_MIX, D_MODEL), D_MIX ** -0.5)
    inp['rwkv_conv'] = jnp.array([0.25, 1.0, 0.25], jnp.float32)[None, :, None] + nrm((DEPTH, 3, 3 * D_RWKV), 0.05)
    inp['rwkv_w0'] = -0.5 + nrm((DEPTH, 2, D_RWKV), 0.5)
    inp['rwkv_w_up'] = nrm((DEPTH, 2, LORA_W, D_RWKV), 0.5 * LORA_W ** -0.5)
    inp['rwkv_a0'] = nrm((DEPTH, 2, D_RWKV), 0.5)
    inp['rwkv_a_up'] = nrm((DEPTH, 2, LORA_A, D_RWKV), 0.5 * LORA_A ** -0.5)
    inp['rwkv_k_k'] = 0.85 + nrm((DEPTH, D_RWKV), 0.05)
    inp['rwkv_k_a'] = 1.0 + nrm((DEPTH, D_RWKV), 0.05)
    inp['rwkv_r_k'] = nrm((DEPTH, N_RWKV, HEAD_DIM), 0.1)
    inp['rwkv_ln_w'] = 1.0 + nrm((DEPTH, D_RWKV), 0.02)
    inp['rwkv_ln_b'] = nrm((DEPTH, D_RWKV), 0.02)
    inp['na_q_norm'] = 1.0 + nrm((DEPTH, HEAD_DIM), 0.02)
    inp['na_k_norm'] = 1.0 + nrm((DEPTH, HEAD_DIM), 0.02)
    inp['na_rpb'] = nrm((DEPTH, N_NA, 2 * NA_ROWS - 1, 2 * NA_COLS - 1), 0.5)
    inp['mla_cq_norm'] = 1.0 + nrm((DEPTH, MLA_Q_RANK), 0.02)
    inp['mla_ckv_norm'] = 1.0 + nrm((DEPTH, MLA_KV_RANK), 0.02)
    inp['mla_w_uq'] = nrm((DEPTH, MLA_Q_RANK, N_MLA * (MLA_NOPE + MLA_ROPE)), MLA_Q_RANK ** -0.5)
    inp['mla_w_uk'] = nrm((DEPTH, MLA_KV_RANK, N_MLA * MLA_NOPE), MLA_KV_RANK ** -0.5)
    inp['mla_w_uv'] = nrm((DEPTH, MLA_KV_RANK, N_MLA * MLA_V), MLA_KV_RANK ** -0.5)
    inp['mla_q_norm'] = 1.0 + nrm((DEPTH, MLA_NOPE + MLA_ROPE), 0.02)
    inp['mla_k_norm'] = 1.0 + nrm((DEPTH, MLA_NOPE + MLA_ROPE), 0.02)
    return inp

def reference(x_prompt, x_sample, state_rwkv, cache_na_k, cache_na_v, cache_mla_ckv, cache_mla_krope,
              c, c_ctx, w_mod, b_mod, norm_w, w_in, w_out, rwkv_conv, rwkv_w0, rwkv_w_up, rwkv_a0,
              rwkv_a_up, rwkv_k_k, rwkv_k_a, rwkv_r_k, rwkv_ln_w, rwkv_ln_b, na_q_norm, na_k_norm, na_rpb,
              mla_cq_norm, mla_ckv_norm, mla_w_uq, mla_w_uk, mla_w_uv, mla_q_norm, mla_k_norm):
    P = dict(w_mod=w_mod, b_mod=b_mod, norm_w=norm_w, w_in=w_in, w_out=w_out, rwkv_conv=rwkv_conv,
             rwkv_w0=rwkv_w0, rwkv_w_up=rwkv_w_up, rwkv_a0=rwkv_a0, rwkv_a_up=rwkv_a_up,
             rwkv_k_k=rwkv_k_k, rwkv_k_a=rwkv_k_a, rwkv_r_k=rwkv_r_k, rwkv_ln_w=rwkv_ln_w,
             rwkv_ln_b=rwkv_ln_b, na_q_norm=na_q_norm, na_k_norm=na_k_norm, na_rpb=na_rpb,
             mla_cq_norm=mla_cq_norm, mla_ckv_norm=mla_ckv_norm, mla_w_uq=mla_w_uq,
             mla_w_uk=mla_w_uk, mla_w_uv=mla_w_uv, mla_q_norm=mla_q_norm, mla_k_norm=mla_k_norm)
    xp = x_prompt
    st = []
    for l in range(DEPTH):
        xp, s_l = context_layer(xp, c_ctx, l, P)
        st.append(s_l)
    new_state_rwkv = jnp.stack([s[0] for s in st], 1).astype(x_prompt.dtype)
    new_cache_na_k = jnp.stack([s[1] for s in st], 1)
    new_cache_na_v = jnp.stack([s[2] for s in st], 1)
    new_cache_mla_ckv = jnp.stack([s[3] for s in st], 1)
    new_cache_mla_krope = jnp.stack([s[4] for s in st], 1)
    xs = x_sample
    for l in range(DEPTH):
        xs = latent_layer(xs, c, state_rwkv[:, l], cache_na_k[:, l], cache_na_v[:, l],
                          cache_mla_ckv[:, l], cache_mla_krope[:, l], l, P)
    return (xp, xs, new_state_rwkv, new_cache_na_k, new_cache_na_v, new_cache_mla_ckv, new_cache_mla_krope)


_drawn_inputs = setup_inputs


def setup_inputs(seed=0):
    import zlib

    import numpy as np

    out = dict(_drawn_inputs(seed))
    spreads = {}
    factors = {'state_rwkv': 8.0,
     'cache_na_k': 6.764,
     'cache_na_v': 5.441,
     'cache_mla_ckv': 8.0,
     'cache_mla_krope': 8.0,
     'rwkv_ln_w': 8.0,
     'rwkv_ln_b': 8.0,
     'na_q_norm': 8.0,
     'na_k_norm': 3.041,
     'na_rpb': 64.0,
     'mla_cq_norm': 8.0,
     'mla_ckv_norm': 2.778,
     'mla_w_uq': 2.717,
     'mla_w_uk': 3.079,
     'mla_q_norm': 8.0,
     'mla_k_norm': 8.0}
    for name, (base, spread) in spreads.items():
        noise = np.random.default_rng([zlib.crc32(name.encode()), seed]).standard_normal(out[name].shape)
        drawn = base * np.exp(spread * noise) if base else spread * noise
        out[name] = __import__('jax').numpy.asarray(drawn.astype(out[name].dtype))
    for name, factor in factors.items():
        out[name] = (out[name] * factor).astype(out[name].dtype)
    return out
```

```python
from contextlib import ExitStack, contextmanager

import numpy as np

import concourse.bass as bass
from concourse import mybir

F32 = mybir.dt.float32
ACT = mybir.ActivationFunctionType
ALU = mybir.AluOpType
AX = mybir.AxisListType.X

P = 128
D = 1024
KD = D // P
DEPTH = 2
CTX = 128
LAT = 2048
TOK = CTX + LAT
NT = TOK // P
PAST = 256
GRID = 64
HD = 64
N_RWKV, N_NA, N_MLA = 4, 6, 6
D_RWKV, D_NA, D_MLA = N_RWKV * HD, N_NA * HD, N_MLA * HD
LORA = 64
Q_RANK, KV_RANK, ROPE = 256, 128, 32
MLA_D = HD + ROPE
NA_ROWS, NA_COLS = 8, 16
EPS = 1e-6
GN_EPS = 64e-5
NEG = -1e30
MLA_SCALE = MLA_D ** -0.5
NA_SCALE = HD ** -0.5

WIDTHS = dict(r=D_RWKV, k=D_RWKV, v=D_RWKV, wd=LORA, ad=LORA, gr=D_RWKV, qn=D_NA, kn=D_NA, vn=D_NA,
              gn=D_NA, cq=Q_RANK, ckv=KV_RANK, krope=ROPE, gm=D_MLA)
COL = {}
_at = 0
for _name, _w in WIDTHS.items():
    COL[_name] = _at
    _at += _w
D_PROJ = _at
CHUNK = 512
N_CHUNK = -(-D_PROJ // CHUNK)
TURN_RWKV = [(COL["r"] + P * i, P) for i in range(7)]
TURN_ATTN = [(COL["qn"] + P * i, P) for i in range(6)] + [(COL["cq"] + P * i, P) for i in range(3)]
TURNS = TURN_RWKV + TURN_ATTN
CTX_COL = 1
LAT_COL = CTX_COL + CTX + 2
FEAT_W = LAT_COL + LAT + 1
NORM_W = 2 * HD + Q_RANK + KV_RANK


class Core:

    def __init__(self, nc, dram):
        self.nc, self.dram = nc, dram
        self.turn = {name: self.sem(f"{name}_turn") for name in ("pe", "act", "dve", "pool", "sp")}

    def sem(self, name):
        return self.nc.alloc_semaphore(name)

    @contextmanager
    def phase(self):
        before = self.nc.snapshot_sems()
        yield
        self.nc.clear_and_free_semaphores(self.nc.allocated_since(before))
        self.nc.all_engine_barrier()

    def hold(self, eng, who):
        eng.sem_inc(self.turn[who], 1)


def phase_modulation(core):
    nc, d, hold = core.nc, core.dram, core.hold
    n_pair = 3 * D // (2 * CHUNK)
    with ExitStack() as mem:
        def sb(name, shape):
            return mem.enter_context(nc.sbuf_tensor(name, shape, F32))
        cond = sb("m_cond", [P, KD, 2])
        half = sb("m_half", [P, KD, 2])
        silu = sb("m_silu", [P, KD, 2])
        wm = sb("m_w", [P, 2, KD, CHUNK])
        bm = sb("m_b", [2, DEPTH * 3 * D])
        row = sb("m_row", [2, 2, CHUNK])
        zero = sb("m_zero", [P, 7, 2])
        ps = mem.enter_context(nc.psum_tensor("m_ps", [P, 2, CHUNK], F32))
        cond_in, tanh_done, silu_done = core.sem("m_cond_in"), core.sem("m_tanh_done"), core.sem("m_silu_done")
        w_in, bias_in = [core.sem("m_w0_in"), core.sem("m_w1_in")], core.sem("m_bias_in")
        mm_done, row_done = core.sem("m_mm_done"), core.sem("m_row_done")
        row_out = [core.sem("m_row0_out"), core.sem("m_row1_out")]
        zero_done, misc_out = core.sem("m_zero_done"), core.sem("m_misc_out")
        with nc.Block() as block:
            @block.sync
            def _(sp):
                sp.dma_start(cond[:, :, :], d["cond"]).then_inc(cond_in, 16)
                with sp.Fori(0, DEPTH) as l:
                    with sp.Fori(0, n_pair) as j:
                        for b in range(2):
                            sp.wait_ge(mm_done, l * 6 + j * 2 + b + 1)
                            hold(sp, "sp")
                            cols = bass.ds(j * (2 * CHUNK) + b * CHUNK, CHUNK)
                            sp.dma_start(wm[:, b, :, :], d["w_mod"][bass.ds(l, 1), :, cols]
                                         .rearrange("a (k p) n -> p (a k) n", p=P)).then_inc(w_in[b], 16)

            @block.gpsimd
            def _(pool):
                pool.memset(zero[:, :, :], 0.0).then_inc(zero_done, 1)
                pool.dma_start(bm[0:2, :], d["b_mod"]).then_inc(bias_in, 16)
                pool.dma_start(d["stream"][0:TOK, :], d["x"]).then_inc(misc_out, 16)
                pool.wait_ge(zero_done, 1)
                fr = d["feat_rwkv"].rearrange("(c p) n -> p c n", p=P)
                with nc.allow_non_contiguous_dma(reason="single zero columns"):
                    for c, n in ((0, 1), (CTX_COL + CTX, 2), (FEAT_W - 1, 1)):
                        pool.dma_start(fr[:, :, c:c + n], zero[:, :, 0:n]).then_inc(misc_out, 16)
                pool.wait_ge(misc_out, 64)

            @block.scalar
            def _(act):
                act.wait_ge(cond_in, 16)
                nc.scalar.activation(half[:, :, :], cond[:, :, :], ACT.Tanh, scale=0.5).then_inc(tanh_done, 1)
                with act.Fori(0, DEPTH) as l:
                    with act.Fori(0, n_pair) as j:
                        for b in range(2):
                            act.wait_ge(row_done, l * 6 + j * 2 + b + 3)
                            hold(act, "act")
                            act.dma_start(d["mod_rows"][bass.ts(l, 2), bass.ds(j * (2 * CHUNK) + b * CHUNK, CHUNK)],
                                          row[:, b, :]).then_inc(row_out[b], 16)
                for b in range(2):
                    act.wait_ge(row_out[b], 16 * (DEPTH * n_pair + 1))

            @block.vector
            def _(dve):
                dve.sem_inc(mm_done, 2)
                dve.sem_inc(row_done, 2)
                for b in range(2):
                    dve.sem_inc(row_out[b], 16)
                dve.wait_ge(tanh_done, 1)
                nc.vector.tensor_scalar(half[:, :, :], half[:, :, :], 0.5, 0.5, ALU.mult, ALU.add)
                dve.drain()
                nc.vector.tensor_tensor(silu[:, :, :], half[:, :, :], cond[:, :, :], ALU.mult).then_inc(silu_done, 1)
                dve.wait_ge(bias_in, 16)
                with dve.Fori(0, DEPTH) as l:
                    with dve.Fori(0, n_pair) as j:
                        for b in range(2):
                            dve.wait_ge(mm_done, l * 6 + j * 2 + b + 3)
                            dve.wait_ge(row_out[b], l * 48 + j * 16 + 16)
                            hold(dve, "dve")
                            nc.vector.tensor_tensor(row[:, b, :], ps[0:2, b, :],
                                                    bm[:, bass.ds(l * (3 * D) + j * (2 * CHUNK) + b * CHUNK, CHUNK)],
                                                    ALU.add).then_inc(row_done, 1)

            @block.tensor
            def _(pe):
                pe.wait_ge(silu_done, 1)
                with pe.Fori(0, DEPTH) as l:
                    with pe.Fori(0, n_pair) as j:
                        for b in range(2):
                            pe.wait_ge(w_in[b], l * 48 + j * 16 + 16)
                            pe.wait_ge(row_done, l * 6 + j * 2 + b + 1)
                            hold(pe, "pe")
                            for k in range(KD):
                                mm = nc.tensor.matmul(ps[0:2, b, :], silu[:, k, :], wm[:, b, k, :],
                                                      start=(k == 0), stop=(k == KD - 1))
                            mm.then_inc(mm_done, 1)


class Tile:

    def __init__(self, t, n, row, col, h, prev=None):
        self.t, self.n, self.row, self.col, self.h, self.p, self.prev = t, n, row, col, h, t % 2, prev


def over_tiles(eng, body):
    def fixed(t, prev):
        return Tile(t, t, t * P, LAT_COL + (t - 1) * P if t else CTX_COL, t // 2, prev)

    def looped(t, j):
        return Tile(t, j * 2 + t, j * (2 * P) + t * P, j * (2 * P) + (LAT_COL + (t - 1) * P), j + t // 2)
    prev = None
    for t in (0, 1, 2):
        prev = fixed(t, prev)
        body(prev)
    with eng.Fori(0, (NT - 5) // 2) as j:
        for t in (3, 4):
            tile = looped(t, j)
            tile.prev = looped(t - 1, j)
            body(tile)
    prev = fixed(NT - 3, None)
    for t in (NT - 2, NT - 1):
        prev = fixed(t, prev)
        body(prev)
    return prev


def of_parity(tile, each):
    return tile.h * each


def phase_projection(core, l):
    nc, d, hold = core.nc, core.dram, core.hold
    with ExitStack() as mem:
        def sb(name, shape):
            return mem.enter_context(nc.sbuf_tensor(name, shape, F32))
        w = sb("a_w", [P, KD, D_PROJ])
        norm_wt = sb("a_norm_wt", [P, NORM_W])
        mod = sb("a_mod", [P, 2, 2, KD])
        nw = sb("a_nw", [P, KD])
        ident = sb("a_ident", [P, P])
        eps = sb("a_eps", [P, 1])
        x = sb("a_x", [P, 2, D])
        xn = sb("a_xn", [P, D])
        xstat = sb("a_xstat", [P, 3])
        sq = sb("a_sq", [P, D])
        stat = sb("a_stat", [P, 3, 14])
        hT = sb("a_hT", [P, KD, P])
        proj = sb("a_proj", [P, 2, D_PROJ])
        fT = sb("a_fT", [P, 2, len(TURNS), P])
        ps_x = [mem.enter_context(nc.psum_tensor(f"a_ps_x{i}", [P, 4, P], F32)) for i in range(2)]
        ps_p = [mem.enter_context(nc.psum_tensor(f"a_ps_p{i}", [P, CHUNK], F32)) for i in range(4)]
        ps_t = [mem.enter_context(nc.psum_tensor(f"a_ps_t{i}", [P, 4, P], F32)) for i in range(2)]
        const_in = core.sem("a_const_in")
        w_in = [core.sem(f"a_w{c}_in") for c in range(N_CHUNK)]
        scale_done, eps_done = core.sem("a_scale_done"), core.sem("a_eps_done")
        x_in = [core.sem("a_x0_in"), core.sem("a_x1_in")]
        x_stat, xn_done, xT_done, hT_done = (core.sem(f"a_{n}") for n in ("x_stat", "xn_done", "xT_done", "hT_done"))
        mm_done, proj_done = core.sem("a_mm_done"), core.sem("a_proj_done")
        sq_done, sum_done, root_done, norm_done = (core.sem(f"a_{n}") for n in ("sq_done", "sum_done", "root_done", "norm_done"))
        turn_done, fT_done = core.sem("a_turn_done"), core.sem("a_fT_done")
        tok_out = [core.sem("a_tok0_out"), core.sem("a_tok1_out")]
        feat_out = [core.sem("a_feat0_out"), core.sem("a_feat1_out")]
        cache_out = core.sem("a_cache_out")
        groups = [range(g, min(g + 4, len(TURNS))) for g in range(0, len(TURNS), 4)]
        ng = len(groups)
        each_tok, each_feat = 5 * 16, 2 * 16
        edges = [(c * CHUNK, min((c + 1) * CHUNK, D_PROJ)) for c in range(N_CHUNK)]
        stream_row = l * TOK

        with nc.Block() as block:
            @block.sync
            def _(sp):
                sp.dma_start(ident[:, :], d["ident"]).then_inc(const_in, 16)
                sp.dma_start(norm_wt[:, :], d["norm_rows"][bass.ds(l, 1), :].broadcast_to([P, NORM_W])).then_inc(const_in, 16)
                with nc.allow_non_contiguous_dma(reason="vectors to one element for each partition"):
                    sp.dma_start(nw[:, :], d["norm_w"][bass.ds(l, 1), :].rearrange("a (k p) -> p (a k)", p=P)).then_inc(const_in, 16)
                    for g in range(2):
                        for s in range(2):
                            sp.dma_start(mod[:, g, s, :], d["mod_rows"][bass.ds(l * 2 + g, 1), s * D:(s + 1) * D]
                                         .rearrange("a (k p) -> p (a k)", p=P)).then_inc(const_in, 16)
                sp.dma_start(x[:, 0, :], d["stream"][bass.ds(stream_row, P), :]).then_inc(x_in[0], 16)
                for c, (lo, hi) in enumerate(edges):
                    sp.dma_start(w[:, :, lo:hi], d["w_in"][bass.ds(l, 1), :, lo:hi]
                                 .rearrange("a (k p) n -> p (a k) n", p=P)).then_inc(w_in[c], 16)

                def store_features(tile):
                    sp.wait_ge(fT_done, tile.n * ng + ng)
                    hold(sp, "sp")
                    f_rwkv = d["feat_rwkv"].rearrange("(c p) n -> p c n", p=P)[:, :, bass.ds(tile.col, P)]
                    f_attn = d["feat_attn"].rearrange("(c p) n -> p c n", p=P)[:, :, bass.ds(tile.row, P)]
                    sp.dma_start(f_rwkv, fT[:, tile.p, 0:7, :]).then_inc(feat_out[tile.p], 16)
                    sp.dma_start(f_attn, fT[:, tile.p, 7:16, :]).then_inc(feat_out[tile.p], 16)
                    if tile.t == 0:
                        for name, lo, hi in (("new_k", COL["kn"], COL["vn"]), ("new_v", COL["vn"], COL["gn"]),
                                             ("new_ckv", COL["ckv"], COL["krope"]), ("new_krope", COL["krope"], COL["gm"])):
                            sp.dma_start(d[name][bass.ts(l, CTX), :], proj[:, 0, lo:hi]).then_inc(cache_out, 16)

                def body(tile):
                    if tile.t < NT - 1:
                        if tile.t > 0:
                            sp.wait_ge(xn_done, tile.n)
                            hold(sp, "sp")
                        sp.dma_start(x[:, 1 - tile.p, :], d["stream"][bass.ds(stream_row + tile.row + P, P), :])\
                            .then_inc(x_in[1 - tile.p], 16)
                    if tile.prev:
                        store_features(tile.prev)
                    sp.wait_ge(proj_done, tile.n * N_CHUNK + N_CHUNK)
                    hold(sp, "sp")
                    gate = d["gate_tok"][bass.ds(tile.row, P), :]
                    for lo, hi, to in ((COL["gr"], COL["qn"], gate[:, 0:D_RWKV]),
                                       (COL["gn"], COL["cq"], gate[:, D_RWKV:D_RWKV + D_NA]),
                                       (COL["gm"], D_PROJ, gate[:, D_RWKV + D_NA:D]),
                                       (COL["vn"], COL["gn"], d["vn_tok"][bass.ds(tile.row, P), :]),
                                       (COL["krope"], COL["gm"], d["krope_tok"][bass.ds(tile.row, P), :])):
                        sp.dma_start(to, proj[:, tile.p, lo:hi]).then_inc(tok_out[tile.p], 16)

                store_features(over_tiles(sp, body))
                for p in range(2):
                    n = (NT + 1 - p) // 2
                    sp.wait_ge(tok_out[p], n * each_tok)
                    sp.wait_ge(feat_out[p], n * each_feat)
                sp.wait_ge(cache_out, 64)

            @block.scalar
            def _(act):
                def x_root(t, p, n, before):
                    act.wait_ge(x_in[p], before + 16)
                    hold(act, "act")
                    if t > 0:
                        act.wait_ge(xn_done, n)
                        hold(act, "act")
                    nc.scalar.activation(sq[:, :], x[:, p, :], ACT.Square, accum_out=xstat[:, 0:1])
                    act.drain()
                    nc.scalar.activation(xstat[:, 1:2], xstat[:, 0:1], ACT.Sqrt, scale=1.0 / D,
                                         bias=eps[:, :]).then_inc(x_stat, 1)

                def norm_roots(tile):
                    pj = proj[:, tile.p, :]
                    nc.scalar.activation(sq[:, 0:2 * D_NA], pj[:, COL["qn"]:COL["vn"]], ACT.Square).then_inc(sq_done, 1)
                    act.wait_ge(sum_done, tile.n + 1)
                    hold(act, "act")
                    nc.scalar.activation(sq[:, 0:Q_RANK], pj[:, COL["cq"]:COL["ckv"]], ACT.Square, accum_out=stat[:, 0, 12:13])
                    act.drain()
                    nc.scalar.activation(sq[:, 0:KV_RANK], pj[:, COL["ckv"]:COL["krope"]], ACT.Square, accum_out=stat[:, 0, 13:14])
                    act.drain()
                    for lo, hi, width in ((0, 12, HD), (12, 13, Q_RANK), (13, 14, KV_RANK)):
                        root = nc.scalar.activation(stat[:, 1, lo:hi], stat[:, 0, lo:hi], ACT.Sqrt, scale=1.0 / width, bias=eps[:, :])
                    root.then_inc(root_done, 1)
                    act.drain()

                def evacuate(tile, c):
                    lo, hi = edges[c]
                    if c == 0 and tile.t > 1:
                        act.wait_ge(tok_out[tile.p], of_parity(tile, each_tok))
                        act.wait_ge(turn_done, tile.n * ng - ng)
                        act.wait_ge(cache_out, 64)
                        hold(act, "act")
                    act.wait_ge(mm_done, tile.n * N_CHUNK + (c + 1))
                    hold(act, "act")
                    nc.scalar.activation(proj[:, tile.p, lo:hi], ps_p[c % 4][:, 0:hi - lo], ACT.Copy).then_inc(proj_done, 1)

                def body(tile):
                    if tile.prev:
                        norm_roots(tile.prev)
                    for c in range(4):
                        evacuate(tile, c)
                    if tile.t < NT - 1:
                        q = Tile(tile.t + 1, 0, 0, 0, tile.h + tile.p)
                        x_root(1, 1 - tile.p, tile.n + 1, of_parity(q, 16))
                        act.drain()
                    for c in range(4, N_CHUNK):
                        evacuate(tile, c)
                    act.drain()

                act.wait_ge(eps_done, 1)
                x_root(0, 0, 0, 0)
                act.drain()
                norm_roots(over_tiles(act, body))

            @block.vector
            def _(dve):
                def normalise_x(p, n):
                    dve.wait_ge(x_stat, n + 1)
                    hold(dve, "dve")
                    nc.vector.reciprocal(xstat[:, 2:3], xstat[:, 1:2])
                    dve.drain()
                    nc.vector.tensor_scalar(xn[:, :], x[:, p, :], xstat[:, 2:3], None, ALU.mult).then_inc(xn_done, 1)

                def modulate(tile):
                    g = 1 if tile.t == 0 else 0
                    for k in range(KD):
                        if k % 4 == 0:
                            dve.wait_ge(xT_done, tile.n * 2 + (k // 4 + 1))
                            hold(dve, "dve")
                        nc.vector.tensor_scalar(hT[:, k, :], ps_x[k // 4][:, k % 4, :], mod[:, g, 1, k:k + 1],
                                                mod[:, g, 0, k:k + 1], ALU.mult, ALU.add).then_inc(hT_done, 1)

                def norm_and_turn(tile):
                    pj = proj[:, tile.p, :]
                    dve.wait_ge(sq_done, tile.n + 1)
                    hold(dve, "dve")
                    nc.vector.tensor_reduce(stat[:, 0, 0:12], sq[:, 0:2 * D_NA].rearrange("p (h e) -> p h e", e=HD),
                                            AX, ALU.add).then_inc(sum_done, 1)
                    dve.wait_ge(root_done, tile.n + 1)
                    hold(dve, "dve")
                    nc.vector.reciprocal(stat[:, 2, :], stat[:, 1, :])
                    dve.drain()
                    qk = pj[:, COL["qn"]:COL["vn"]].rearrange("p (h e) -> p h e", e=HD)
                    nc.vector.tensor_tensor(qk, qk, stat[:, 2, 0:12].unsqueeze(2).broadcast_to([P, 12, HD]), ALU.mult)
                    for lo, hi, s, wl in ((COL["cq"], COL["ckv"], 12, 2 * HD), (COL["ckv"], COL["krope"], 13, 2 * HD + Q_RANK)):
                        nc.vector.scalar_tensor_tensor(out=pj[:, lo:hi], in0=pj[:, lo:hi], scalar=stat[:, 2, s:s + 1],
                                                       in1=norm_wt[:, wl:wl + hi - lo], op0=ALU.mult, op1=ALU.mult)
                    dve.drain()
                    for i in range(2):
                        part = qk[:, 6 * i:6 * i + 6, :]
                        last = nc.vector.tensor_tensor(part, part, norm_wt[:, HD * i:HD * i + HD].unsqueeze(1)
                                                       .broadcast_to([P, 6, HD]), ALU.mult)
                    last.then_inc(norm_done, 1)
                    for g, blocks in enumerate(groups):
                        if g == 0 and tile.t > 1:
                            dve.wait_ge(feat_out[tile.p], of_parity(tile, each_feat))
                            hold(dve, "dve")
                        dve.wait_ge(turn_done, tile.n * ng + (g + 1))
                        hold(dve, "dve")
                        nc.vector.tensor_copy(fT[:, tile.p, blocks[0]:blocks[-1] + 1, :], ps_t[g % 2][:, :, :]).then_inc(fT_done, 1)

                def body(tile):
                    modulate(tile)
                    if tile.prev:
                        norm_and_turn(tile.prev)
                    if tile.t < NT - 1:
                        normalise_x(1 - tile.p, tile.n + 1)

                nc.vector.memset(eps[:, :], EPS).then_inc(eps_done, 1)
                dve.wait_ge(const_in, 16 * 7)
                for g in range(2):
                    nc.vector.scalar_tensor_tensor(out=mod[:, g, 1, :], in0=mod[:, g, 1, :], scalar=1.0, in1=nw[:, :],
                                                   op0=ALU.add, op1=ALU.mult)
                nc.vector.tensor_scalar(norm_wt[:, 0:HD], norm_wt[:, 0:HD], NA_SCALE, None, ALU.mult)
                dve.drain()
                normalise_x(0, 0)
                norm_and_turn(over_tiles(dve, body))

            @block.tensor
            def _(pe):
                def turn_x(tile):
                    pe.wait_ge(xn_done, tile.n + 1)
                    hold(pe, "pe")
                    if tile.prev:
                        pe.wait_ge(hT_done, tile.n * KD)
                        hold(pe, "pe")
                    for k in range(KD):
                        tr = nc.tensor.transpose(ps_x[k // 4][:, k % 4, :], xn[:, k * P:(k + 1) * P], ident[:, :])
                        if k % 4 == 3:
                            tr.then_inc(xT_done, 1)

                def project(tile, c):
                    lo, hi = edges[c]
                    if tile.t == 0:
                        pe.wait_ge(w_in[c], 16)
                        if c >= 4:
                            pe.wait_ge(proj_done, tile.n * N_CHUNK + (c - 3))
                            hold(pe, "pe")
                    elif c >= 4:
                        pe.wait_ge(proj_done, tile.n * N_CHUNK + (c - 3))
                        hold(pe, "pe")
                    else:
                        pe.wait_ge(proj_done, tile.prev.n * N_CHUNK + (c + 5 if c < 3 else c + 1))
                        hold(pe, "pe")
                    for k in range(KD):
                        if c == 0:
                            pe.wait_ge(hT_done, tile.n * KD + (k + 1))
                            hold(pe, "pe")
                        mm = nc.tensor.matmul(ps_p[c % 4][:, 0:hi - lo], hT[:, k, :], w[:, k, lo:hi],
                                              start=(k == 0), stop=(k == KD - 1))
                    mm.then_inc(mm_done, 1)

                def turn_out(tile):
                    pe.wait_ge(norm_done, tile.n + 1)
                    hold(pe, "pe")
                    for g, blocks in enumerate(groups):
                        if g < 2:
                            if tile.t > 0:
                                pe.wait_ge(fT_done, tile.n * ng - (1 - g))
                                hold(pe, "pe")
                        else:
                            pe.wait_ge(fT_done, tile.n * ng + (g - 1))
                            hold(pe, "pe")
                        for i, blk in enumerate(blocks):
                            lo, width = TURNS[blk]
                            tr = nc.tensor.transpose(ps_t[g % 2][:, i, :], proj[:, tile.p, lo:lo + width], ident[:, :])
                        tr.then_inc(turn_done, 1)

                def body(tile):
                    turn_x(tile)
                    for c in range(4):
                        project(tile, c)
                    if tile.prev:
                        turn_out(tile.prev)
                    for c in range(4, N_CHUNK):
                        project(tile, c)

                pe.wait_ge(const_in, 16 * 7)
                turn_out(over_tiles(pe, body))


C = 64
DECAY_AMP = float(np.exp(-0.5))
KK_MIN = 1e-12
M_STRICT_T, M_INCL_T, M_EYE = 0, 1, 2
W_LEV1_T, W_EYE, W_LEV, N_WIDE = 0, 1, 2, 8
N_FEAT_PAR = 32


class Step:

    def __init__(self, s, n, col, row):
        self.s, self.n, self.col, self.row, self.p = s, n, col, row, s % 2


def over_steps(eng, body):
    def fixed(s):
        if s == 0:
            return Step(0, 0, (CTX_COL - 1,) * 2, (0, 0))
        return Step(s, s, (LAT_COL - 1 + (s - 1) * P, LAT_COL - 1 + (NQ - s) * P), (CTX + (s - 1) * P, CTX + (NQ - s) * P))

    def looped(s, j):
        return Step(s, j * 2 + s,
                    (j * (2 * P) + (LAT_COL - 1 + (s - 1) * P), j * (-2 * P) + (LAT_COL - 1 + (NQ - s) * P)),
                    (j * (2 * P) + (CTX + (s - 1) * P), j * (-2 * P) + (CTX + (NQ - s) * P)))
    body(fixed(0), fixed(1))
    with eng.Fori(0, (NT - 3) // 2) as j:
        for s in (1, 2):
            body(looped(s, j), looped(s + 1, j))
    body(fixed(NT - 2), fixed(NT - 1))
    body(fixed(NT - 1), None)


def phase_scans(core, l):
    nc, d, hold = core.nc, core.dram, core.hold
    SLOTS = [(e, dh, pz) for e in range(2) for dh in range(4) for pz in range(2)]
    with ExitStack() as mem:
        def sb(name, shape):
            return mem.enter_context(nc.sbuf_tensor(name, shape, F32))

        def pair(name, shape):
            return [sb(f"{name}{i}", shape) for i in range(2)]
        ident = sb("s_ident", [P, P])
        masks = sb("s_masks", [P, 3, 4, C])
        wide = sb("s_wide", [P, N_WIDE, 2, P])
        head_ones = sb("s_head_ones", [P, P])
        head_sel = sb("s_head_sel", [P, 2])
        half_sel = sb("s_half_sel", [P, 2, C])
        reset = sb("s_reset", [P, 4 * P])
        par = sb("s_par", [P, N_FEAT_PAR])
        up = sb("s_up", [P, 2, D_RWKV])
        raw = sb("s_raw", [P, 2, 6, P + 2])
        lora = sb("s_lora", [P, 2, P])
        rkv = pair("s_rkv", [P, 3, 2, 2, P])
        tap = sb("s_tap", [P, 3, 6, P])
        kkr = sb("s_kkr", [P, 4, P])
        sq = sb("s_sq", [P, 4 * P])
        wz, az = sb("s_wz", [P, 4, P]), sb("s_az", [P, 4, P])
        rn = sb("s_rn", [P, 4 * P])
        lw, cum = sb("s_lw", [P, 4 * P]), sb("s_cum", [P, 4 * P])
        g, gx, cg = (sb(f"s_{n}", [P, 2, 2 * P]) for n in ("g", "gx", "cg"))
        kd, tmp, nb = (sb(f"s_{n}", [P, 4, P]) for n in ("kd", "tmp", "nb"))
        rT, aT, bT, kT, bhT, khT, rkT = (pair(f"s_{n}", [P, 4, P]) for n in ("rT", "aT", "bT", "kT", "bhT", "khT", "rkT"))
        decayC = pair("s_decayC", [P, 4, 2])
        Araw, X, XT, YT, Pm = (sb(f"s_{n}", [P, 2, 4, P]) for n in ("Araw", "X", "XT", "YT", "P"))
        lev = sb("s_lev", [P, 5, 2, 4, P])
        AkT, RbT, RkT, Z, U, GT, QT, WI, M = (
            sb(f"s_{n}", [P, 2, 4, C]) for n in ("AkT", "RbT", "RkT", "Z", "U", "GT", "QT", "WI", "M"))
        A_tok, B_tok, K_tok, V_tok = (sb(f"s_{n}_tok", [P, 4, 2, C]) for n in "ABKV")
        R_wide = sb("s_R_wide", [P, 4, 2, P])
        small = sb("s_small", [P, 16])
        y_tok, bonus = sb("s_y_tok", [P, 4, 2, C]), sb("s_bonus", [P, 4, 2, C])
        ps = mem.enter_context(nc.psum_tensor("s_ps", [P, 8, CHUNK], F32))

        def slots(i):
            return ps[:, i, :].rearrange("p (e h c) -> p e h c", e=2, c=C)

        def mask_pair(op, e, out, src, m):
            view = lambda t: t.rearrange("p (d h) c -> p d h c", d=2)
            return op(view(out[:, e, :, :]), view(src), wide[:, m, :, :].unsqueeze(2).broadcast_to([P, 2, 2, P]))

        sems = {}

        def S(name):
            if name not in sems:
                sems[name] = core.sem(f"s_{name}")
            return sems[name]
        for name in ("const_in", "state_in", "raw_in", "sq_done", "tanh_done", "lora_done", "sum_done", "root_done", "z_read", "za_tanh",
                     "norm_done", "lw_done", "cum_done", "g_done", "exp_done", "ready", "prod_done",
                     "raw_moved", "x_made", "lev_done", "small_done", "small_moved", "tok_done", "tok_moved", "masked", "z_done",
                     "z_moved", "yt_done", "yt_moved_v", "yt_moved_a", "xt_done", "xx_done", "xt_added", "x_added", "pu_done",
                     "p_moved_v", "p_moved_a", "u_moved", "gq_done",
                     "g_moved", "q_moved", "wi_done", "m_done", "m_moved_v", "m_moved_a", "y_done", "y_moved",
                     "bonus_done", "sent", "state_sent", "conv_done", "zeroed"):
            S(name)
        n_const = 10

        with nc.Block() as block:
            @block.sync
            def _(sp):
                sp.dma_start(ident[:, :], d["ident"]).then_inc(S("const_in"), 16)
                sp.dma_start(masks[:, :, :, :], d["masks"]).then_inc(S("const_in"), 16)
                sp.dma_start(wide[:, :, :, :], d["wide_masks"]).then_inc(S("const_in"), 16)
                sp.dma_start(head_ones[:, :], d["head_ones"]).then_inc(S("const_in"), 16)
                sp.dma_start(head_sel[:, :], d["head_sel"]).then_inc(S("const_in"), 16)
                sp.dma_start(half_sel[:, :, :], d["half_sel"]).then_inc(S("const_in"), 16)
                sp.dma_start(reset[:, :], d["reset"]).then_inc(S("const_in"), 16)
                sp.dma_start(par[:, :], d["rwkv_par"][bass.ds(l * P, P), :]).then_inc(S("const_in"), 16)
                for i, name in enumerate(("w_up", "a_up")):
                    sp.dma_start(up[C * i:C * i + C, :, :], d[name][bass.ds(l * C, C), :, :]).then_inc(S("const_in"), 16)

                def load(step):
                    if step.s > 0:
                        sp.wait_ge(S("conv_done"), step.n)
                        sp.wait_ge(S("z_read"), step.n)
                        hold(sp, "sp")
                    f = d["feat_rwkv"].rearrange("(c p) n -> p c n", p=P)
                    for i in range(2):
                        sp.dma_start(raw[:, i, :, :], f[:, 0:6, bass.ds(step.col[i], P + 2)]).then_inc(S("raw_in"), 16)
                        sp.dma_start(lora[:, i, :], f[:, 6, bass.ds(step.col[i] + 1, P)]).then_inc(S("raw_in"), 16)

                def body(step, nxt):
                    if nxt:
                        load(nxt)
                    for name, src, done in (("scan_tok", y_tok, "y_moved"), ("bonus_tok", bonus, "bonus_done")):
                        sp.wait_ge(S(done), step.n + 1)
                        hold(sp, "sp")
                        for i in range(2):
                            sp.dma_start(d[name][bass.ds(step.row[i] + i * TOK, P), :],
                                         src[:, 2 * i:2 * i + 2, :, :].rearrange("p h e c -> p (h e c)")).then_inc(S("sent"), 16)
                    if step.s == 0:
                        sp.wait_ge(S("m_moved_v"), 2)
                        sp.wait_ge(S("m_moved_a"), 2)
                        for i in range(2):
                            rows = M[C * i:C * i + C, :, 2 * i:2 * i + 2, :]
                            sp.dma_start(d["new_state"][bass.ds(l * 2 * C + i * C, C), :, :, :], rows).then_inc(S("state_sent"), 16)
                        sp.wait_ge(S("state_sent"), 32)
                        sp.wait_ge(S("y_done"), step.n + 1)
                        hold(sp, "sp")
                        for i in range(2):
                            rows = M[C * i:C * i + C, :, 2 * i:2 * i + 2, :]
                            sp.dma_start(rows, d["state0"][bass.ds(l * 2 * C + i * C, C), :, :, :]).then_inc(S("state_in"), 16)
                load(Step(0, 0, (CTX_COL - 1,) * 2, (0, 0)))
                over_steps(sp, body)
                sp.wait_ge(S("sent"), 64 * NT)

            @block.gpsimd
            def _(pool):
                tt, ts = nc.gpsimd.tensor_tensor, nc.gpsimd.tensor_scalar

                def flat(t):
                    return t[:, :, :].rearrange("p h n -> p (h n)")

                def convolve(step):
                    pool.wait_ge(S("raw_in"), step.n * 64 + 64)
                    hold(pool, "pool")
                    q = rkv[step.p]
                    for i in range(2):
                        for t in range(3):
                            w = par[:, 6 * t:6 * t + 6].unsqueeze(2).broadcast_to([P, 6, P])
                            tt(tap[:, t, :, :], raw[:, i, :, t:t + P], w, ALU.mult)
                        pool.drain()
                        tt(tap[:, 0, :, :], tap[:, 0, :, :], tap[:, 1, :, :], ALU.add)
                        pool.drain()
                        out = q[:, :, i, :, :]
                        last = tt(out, tap[:, 0, :, :].rearrange("p (a h) n -> p a h n", h=2),
                                  tap[:, 2, :, :].rearrange("p (a h) n -> p a h n", h=2), ALU.add)
                        pool.drain()
                    last.then_inc(S("conv_done"), 1)
                    k_k = par[:, 18:20].unsqueeze(1).unsqueeze(3).broadcast_to([P, 2, 2, P])
                    tt(kkr[:, :, :].rearrange("p (d h) n -> p d h n", d=2), q[:, 1, :, :, :], k_k, ALU.mult)
                    pool.drain()
                    tt(sq[:, :], flat(kkr), flat(kkr), ALU.mult).then_inc(S("sq_done"), 1)

                def decays(step):
                    pool.wait_ge(S("za_tanh"), step.n * 2 + 2)
                    hold(pool, "pool")
                    ts(lw[:, :], flat(wz), -0.5 * DECAY_AMP, -0.5 * DECAY_AMP, ALU.mult, ALU.add).then_inc(S("lw_done"), 1)
                    ts(tmp[:, :, :], az[:, :, :], 0.5, -0.5, ALU.mult, ALU.add)
                    ts(nb[:, :, :], az[:, :, :], 0.5, 0.5, ALU.mult, ALU.add)
                    pool.drain()
                    k_a = par[:, 20:22].unsqueeze(1).unsqueeze(3).broadcast_to([P, 2, 2, P])
                    t4 = tmp[:, :, :].rearrange("p (d h) n -> p d h n", d=2)
                    tt(t4, t4, k_a, ALU.mult)
                    pool.drain()
                    ts(tmp[:, :, :], tmp[:, :, :], 1.0, 1.0, ALU.add, ALU.mult)
                    pool.drain()
                    k = rkv[step.p][:, 1, :, :, :].rearrange("p d h n -> p (d h) n")
                    tt(kd[:, :, :], tmp[:, :, :], k, ALU.mult)
                    pool.drain()
                    r = rkv[step.p][:, 0, :, :, :]
                    r_k = par[:, 22:24].unsqueeze(1).unsqueeze(3).broadcast_to([P, 2, 2, P])
                    tt(t4, r, r_k, ALU.mult)
                    pool.drain()
                    tt(rkT[step.p][:, :, :], tmp[:, :, :], kd[:, :, :], ALU.mult)
                    pool.wait_ge(S("norm_done"), step.n * 2 + 2)
                    hold(pool, "pool")
                    tt(flat(kkr), flat(kkr), rn[:, :], ALU.mult)
                    pool.drain()
                    tt(nb[:, :, :], nb[:, :, :], kkr[:, :, :], ALU.mult)
                    pool.wait_ge(S("cum_done"), step.n + 1)
                    hold(pool, "pool")
                    c3 = cum[:, :].rearrange("p (d q c) -> p d q c", d=2, c=C)
                    l3 = lw[:, :].rearrange("p (d q c) -> p d q c", d=2, c=C)
                    gv, xv, cv = (t[:, :, :].rearrange("p d (q c) -> p d q c", c=C) for t in (g, gx, cg))
                    for i, (less_own, rest) in enumerate(((xv, cv), (cv, xv))):
                        tt(less_own[:, i, :, :], c3[:, i, :, :], l3[:, i, :, :], ALU.subtract)
                        tt(rest[:, i, :, :], c3[:, i, :, C - 1:C].broadcast_to([P, 4, C]), c3[:, i, :, :], ALU.subtract)
                    nc.gpsimd.tensor_copy(gv[:, 0, :, :], c3[:, 0, :, :])
                    pool.drain()
                    tt(gv[:, 1, :, :], xv[:, 1, :, :], l3[:, 1, :, :], ALU.add).then_inc(S("g_done"), 1)

                def scale(step):
                    pool.wait_ge(S("exp_done"), step.n + 1)
                    hold(pool, "pool")
                    p = step.p
                    r = rkv[p][:, 0, :, :, :].rearrange("p d h n -> p (d h n)")
                    eg, ex, ec = (t[:, :, :].rearrange("p d n -> p (d n)") for t in (g, gx, cg))
                    tt(flat(aT[p]), flat(kkr), ex, ALU.mult)
                    tt(flat(bT[p]), flat(nb), cum[:, :], ALU.mult).then_inc(S("ready"), 1)
                    tt(flat(rT[p]), r, eg, ALU.mult)
                    tt(flat(kT[p]), flat(kd), cum[:, :], ALU.mult).then_inc(S("ready"), 1)
                    tt(flat(bhT[p]), flat(nb), ec, ALU.mult)
                    tt(flat(khT[p]), flat(kd), ec, ALU.mult).then_inc(S("ready"), 1)

                def levels(step):
                    pool.wait_ge(S("raw_moved"), step.n + 1)
                    hold(pool, "pool")
                    for j in range(5):
                        for e in range(2):
                            last = mask_pair(lambda o, i, m: tt(o, i, m, ALU.mult), e, lev[:, j, :, :, :], Araw[:, e, :, :], W_LEV + 1 + j)
                        last.then_inc(S("lev_done"), 1)

                def side(step):
                    pool.wait_ge(S("small_moved"), step.n + 1)
                    hold(pool, "pool")
                    w = small[:, 0:8].rearrange("p (e h) -> p e h", e=2)
                    for e in range(2):
                        last = tt(WI[:, e, :, :], masks[:, M_EYE, :, :], w[:, e, :].unsqueeze(2).broadcast_to([P, 4, C]), ALU.mult)
                    last.then_inc(S("wi_done"), 1)
                    pool.wait_ge(S("tok_moved"), step.n * 5 + 2)
                    hold(pool, "pool")
                    if step.s > 0:
                        pool.wait_ge(S("sent"), step.n * 64)
                        hold(pool, "pool")
                    tt(bonus[:, :, :, :].rearrange("p h e c -> p (h e) c"), V_tok[:, :, :, :].rearrange("p h e c -> p (h e) c"),
                       small[:, 8:16].unsqueeze(2).broadcast_to([P, 8, C]), ALU.mult).then_inc(S("bonus_done"), 1)

                def prepare(step):
                    convolve(step)
                    decays(step)
                    scale(step)

                def body(step, nxt):
                    levels(step)
                    side(step)
                    if nxt:
                        prepare(nxt)
                nc.gpsimd.memset(M[:, :, :, :], 0.0).then_inc(S("zeroed"), 1)
                nc.gpsimd.memset(Pm[:, :, :, :], 0.0).then_inc(S("zeroed"), 1)
                nc.gpsimd.memset(R_wide[:, :, :, :], 0.0).then_inc(S("zeroed"), 1)
                pool.wait_ge(S("const_in"), 16 * n_const)
                prepare(Step(0, 0, None, None))
                over_steps(pool, body)

            @block.scalar
            def _(act):
                def lora_tanh(step):
                    act.wait_ge(S("raw_in"), step.n * 64 + 64)
                    hold(act, "act")
                    nc.scalar.activation(lora[0:C, :, :], lora[0:C, :, :], ACT.Tanh).then_inc(S("tanh_done"), 1)

                def gate_tanh(step):
                    act.wait_ge(S("z_read"), step.n + 1)
                    hold(act, "act")
                    for t in (wz, az):
                        nc.scalar.activation(t[:, :, :], t[:, :, :], ACT.Tanh, scale=0.5).then_inc(S("za_tanh"), 1)

                def root(step):
                    act.wait_ge(S("sum_done"), step.n + 1)
                    if step.s > 0:
                        act.wait_ge(S("ready"), step.n * 3)
                    hold(act, "act")
                    nc.scalar.activation(rn[:, :], ps[:, 6, :], ACT.Sqrt).then_inc(S("root_done"), 1)

                def exps(step):
                    act.wait_ge(S("g_done"), step.n + 1)
                    hold(act, "act")
                    ends = cum[:, :].rearrange("p (h z c) -> p h z c", z=2, c=C)[:, :, :, C - 1]
                    nc.scalar.activation(decayC[step.p][:, :, :], ends, ACT.Exp)
                    act.drain()
                    nc.scalar.activation(cum[:, :], g[:, :, :].rearrange("p d n -> p (d n)"), ACT.Exp, scale=-1.0)
                    act.drain()
                    for t in (g, gx, cg):
                        last = nc.scalar.activation(t[:, :, :], t[:, :, :], ACT.Exp)
                    last.then_inc(S("exp_done"), 1)

                def main(step, nxt):
                    n, copy = step.n, lambda o, i: nc.scalar.activation(o, i, ACT.Copy)
                    act.wait_ge(S("prod_done"), n * 5 + 2)
                    hold(act, "act")
                    copy(Araw[:, :, :, :].rearrange("p e h c -> p e (h c)"), ps[:, 4:6, :]).then_inc(S("raw_moved"), 1)
                    act.wait_ge(S("small_done"), n + 1)
                    hold(act, "act")
                    if step.s > 0:
                        act.wait_ge(S("bonus_done"), n)
                        hold(act, "act")
                    copy(small[:, :], ps[:, 7, 0:16]).then_inc(S("small_moved"), 1)
                    for i, (t, b) in enumerate(((A_tok, 6), (V_tok, 7), (B_tok, 4), (K_tok, 5))):
                        act.wait_ge(S("tok_done"), n * 5 + (i + 1))
                        hold(act, "act")
                        nc.scalar.activation(t[:, :, :, :].rearrange("p h e c -> p (h e c)"), ps[:, b, :], ACT.Copy,
                                             scale=-1.0 if i == 0 else 1.0).then_inc(S("tok_moved"), 1)
                    act.wait_ge(S("tok_done"), n * 5 + 5)
                    if step.s == 0:
                        act.wait_ge(S("zeroed"), 3)
                    hold(act, "act")
                    for pz in range(2):
                        t = slice(C * pz, C * pz + C)
                        last = copy(R_wide[t, :, :, t].rearrange("p h e c -> p (h e) c"), ps[t, 6, :].rearrange("p (h c) -> p h c", c=C))
                    last.then_inc(S("tok_moved"), 1)
                    if nxt:
                        lora_tanh(nxt)
                    act.wait_ge(S("z_done"), n + 1)
                    hold(act, "act")
                    copy(Z[:, :, :, :], slots(3)).then_inc(S("z_moved"), 1)
                    for j in range(5):
                        act.wait_ge(S("yt_done"), n * 5 + (j + 1))
                        hold(act, "act")
                        copy(YT[:, 0, :, :].rearrange("p h c -> p (h c)"), ps[:, 0, :]).then_inc(S("yt_moved_a"), 1)
                        if nxt and j == 2:
                            gate_tanh(nxt)
                        if nxt and j == 3:
                            root(nxt)
                    act.wait_ge(S("pu_done"), n * 2 + 1)
                    if step.s == 0:
                        act.wait_ge(S("zeroed"), 3)
                    hold(act, "act")
                    copy(Pm[C:P, :, :, C:P], slots(0)[C:P, :, :, :]).then_inc(S("p_moved_a"), 1)
                    act.wait_ge(S("pu_done"), n * 2 + 2)
                    hold(act, "act")
                    copy(U[:, :, :, :], slots(1)).then_inc(S("u_moved"), 1)
                    act.wait_ge(S("gq_done"), n * 2 + 2)
                    hold(act, "act")
                    copy(QT[:, :, :, :], slots(3)).then_inc(S("q_moved"), 1)
                    for rnd, rows in enumerate((slice(0, C), slice(C, P))):
                        act.wait_ge(S("m_done"), n * 2 + (rnd + 1))
                        hold(act, "act")
                        copy(M[rows, :, 2:4, :], slots(5)[rows, :, 2:4, :]).then_inc(S("m_moved_a"), 1)
                        if nxt and rnd == 0:
                            exps(nxt)
                    act.wait_ge(S("y_done"), n + 1)
                    hold(act, "act")
                    if step.s > 0:
                        act.wait_ge(S("sent"), n * 64)
                        hold(act, "act")
                    copy(y_tok[:, :, :, :].rearrange("p h e c -> p e h c"), slots(4)).then_inc(S("y_moved"), 1)

                first = Step(0, 0, None, None)
                lora_tanh(first)
                gate_tanh(first)
                root(first)
                exps(first)
                over_steps(act, main)

            @block.vector
            def _(dve):
                tt = nc.vector.tensor_tensor

                def add_biases(step):
                    dve.wait_ge(S("lora_done"), step.n + 1)
                    hold(dve, "dve")
                    for t, b, c in ((wz, 6, 24), (az, 7, 28)):
                        last = tt(t[:, :, :], ps[:, b, :].rearrange("p (h n) -> p h n", h=4),
                                  par[:, c:c + 4].unsqueeze(2).broadcast_to([P, 4, P]), ALU.add)
                    last.then_inc(S("z_read"), 1)

                def norm(step, i):
                    dve.wait_ge(S("root_done"), step.n + 1)
                    hold(dve, "dve")
                    cols = slice(i * 2 * P, (i + 1) * 2 * P)
                    nc.vector.tensor_scalar(rn[:, cols], rn[:, cols], KK_MIN, None, ALU.max)
                    dve.drain()
                    nc.vector.reciprocal(rn[:, cols], rn[:, cols]).then_inc(S("norm_done"), 1)

                def cumulate(step):
                    dve.wait_ge(S("lw_done"), step.n + 1)
                    hold(dve, "dve")
                    nc.vector.tensor_tensor_scan(cum[:, :], reset[:, :], lw[:, :], 0.0, ALU.mult, ALU.add).then_inc(S("cum_done"), 1)

                def main(step, nxt):
                    n = step.n
                    both = lambda m: masks[:, m, :, :].rearrange("p h c -> p (h c)").unsqueeze(1).broadcast_to([P, 2, 4 * C])
                    eh = lambda t: t[:, :, :, :].rearrange("p e h c -> p e (h c)")
                    mul = lambda o, i, m: tt(o, i, m, ALU.mult)
                    add = lambda o, i, m: tt(o, i, m, ALU.add)
                    pairs = lambda t: t[:, :, :, :].rearrange("p e h c -> p e (h c)")
                    dve.wait_ge(S("prod_done"), n * 5 + 1)
                    hold(dve, "dve")
                    for e in range(2):
                        mask_pair(mul, e, XT, ps[:, e, :].rearrange("p (h c) -> p h c", c=P), W_LEV1_T)
                    dve.wait_ge(S("prod_done"), n * 5 + 3)
                    hold(dve, "dve")
                    tt(eh(RbT), ps[:, 6:8, 4 * C:8 * C], both(M_INCL_T), ALU.mult).then_inc(S("masked"), 1)
                    dve.drain()
                    for e in range(2):
                        mask_pair(add, e, XT, XT[:, e, :, :], W_EYE)
                    dve.wait_ge(S("prod_done"), n * 5 + 5)
                    hold(dve, "dve")
                    tt(eh(AkT), ps[:, 2:4, 0:4 * C], both(M_STRICT_T), ALU.mult)
                    tt(eh(RkT), ps[:, 2:4, 4 * C:8 * C], both(M_INCL_T), ALU.mult).then_inc(S("masked"), 1)
                    dve.wait_ge(S("raw_moved"), n + 1)
                    hold(dve, "dve")
                    for e in range(2):
                        mask_pair(mul, e, X, Araw[:, e, :, :], W_LEV)
                    dve.drain()
                    for e in range(2):
                        last = mask_pair(add, e, X, X[:, e, :, :], W_EYE)
                    last.then_inc(S("x_made"), 1)
                    for j in range(5):
                        dve.wait_ge(S("yt_done"), n * 5 + (j + 1))
                        hold(dve, "dve")
                        nc.vector.tensor_copy(YT[:, 1, :, :].rearrange("p h c -> p (h c)"), ps[:, 1, :]).then_inc(S("yt_moved_v"), 1)
                        dve.wait_ge(S("xt_done"), n * 5 + (j + 1))
                        hold(dve, "dve")
                        for e in range(2):
                            row = XT[:, e, :, :].rearrange("p h c -> p (h c)")
                            tt(row, row, ps[:, 2 + e, :], ALU.add).then_inc(S("xt_added"), 1)
                        if j < 4:
                            dve.wait_ge(S("xx_done"), n * 4 + (j + 1))
                            hold(dve, "dve")
                            tt(pairs(X), pairs(X), ps[:, 4:6, :], ALU.add).then_inc(S("x_added"), 1)
                        if nxt and j == 1:
                            add_biases(nxt)
                        if nxt and j == 4:
                            norm(nxt, 0)
                    dve.wait_ge(S("pu_done"), n * 2 + 1)
                    hold(dve, "dve")
                    if step.s == 0:
                        dve.wait_ge(S("zeroed"), 3)
                    nc.vector.tensor_copy(Pm[0:C, :, :, 0:C], slots(0)[0:C, :, :, :]).then_inc(S("p_moved_v"), 1)
                    if nxt:
                        cumulate(nxt)
                        norm(nxt, 1)
                    dve.wait_ge(S("wi_done"), n + 1)
                    dve.wait_ge(S("gq_done"), n * 2 + 1)
                    hold(dve, "dve")
                    tt(GT[:, :, :, :], WI[:, :, :, :], slots(2), ALU.add).then_inc(S("g_moved"), 1)
                    for rnd, rows in enumerate((slice(C, P), slice(0, C))):
                        dve.wait_ge(S("m_done"), n * 2 + (rnd + 1))
                        hold(dve, "dve")
                        nc.vector.tensor_copy(M[rows, :, 0:2, :], slots(5)[rows, :, 0:2, :]).then_inc(S("m_moved_v"), 1)

                dve.wait_ge(S("const_in"), 16 * n_const)
                first = Step(0, 0, None, None)
                add_biases(first)
                norm(first, 0)
                norm(first, 1)
                cumulate(first)
                over_steps(dve, main)

            @block.tensor
            def _(pe):
                mm = nc.tensor.matmul

                def lora_products(step):
                    pe.wait_ge(S("tanh_done"), step.n + 1)
                    hold(pe, "pe")
                    for dh in range(4):
                        for i in range(2):
                            rows = slice(C * i, C * i + C)
                            last = mm(ps[:, 6 + i, dh * P:dh * P + P], up[rows, dh // 2, (dh % 2) * P:(dh % 2) * P + P],
                                      lora[rows, dh // 2, :], start=True, stop=True)
                    last.then_inc(S("lora_done"), 1)

                def norm_sums(step):
                    pe.wait_ge(S("sq_done"), step.n + 1)
                    pe.wait_ge(S("z_read"), step.n + 1)
                    hold(pe, "pe")
                    mm(ps[:, 6, :], head_ones[:, :], sq[:, :], start=True, stop=True).then_inc(S("sum_done"), 1)

                def products(step):
                    n, p = step.n, step.p
                    pe.wait_ge(S("ready"), n * 3 + 1)
                    hold(pe, "pe")
                    if step.s > 0:
                        for name, per in (("p_moved_v", 1), ("p_moved_a", 1), ("u_moved", 1), ("g_moved", 1), ("q_moved", 1), ("y_moved", 1),
                                          ("m_moved_v", 2), ("m_moved_a", 2)):
                            pe.wait_ge(S(name), n * per)
                            hold(pe, "pe")
                    for bank, left, right in ((0, bT[p], aT[p]), (4, aT[p], bT[p])):
                        for e in range(2):
                            k = slice(C * e, C * e + C)
                            for dh in range(4):
                                last = mm(ps[:, bank + e, dh * P:dh * P + P], left[k, dh, :], right[k, dh, :], start=True, stop=True)
                        last.then_inc(S("prod_done"), 1)
                    pe.wait_ge(S("ready"), n * 3 + 2)
                    hold(pe, "pe")
                    for bank, i, left, right in ((6, 1, bT[p], rT[p]), (2, 0, kT[p], aT[p]), (2, 1, kT[p], rT[p])):
                        for e, dh, pz in SLOTS:
                            k, t = slice(C * e, C * e + C), slice(C * pz, C * pz + C)
                            last = mm(ps[t, bank + e, (4 * i + dh) * C:(4 * i + dh + 1) * C], left[k, dh, t], right[k, dh, t],
                                      start=True, stop=True)
                        last.then_inc(S("prod_done"), 1)
                    pe.wait_ge(S("masked"), n * 2 + 1)
                    hold(pe, "pe")
                    for pz in range(2):
                        for e in range(2):
                            mm(ps[C * pz:C * pz + C, 7, 4 * e:4 * e + 4], half_sel[:, e, :], decayC[p][:, :, pz], start=True, stop=True)
                    for dh in range(4):
                        last = mm(ps[:, 7, 8 + 2 * dh:10 + 2 * dh], rkT[p][:, dh, :], head_sel[:, :], start=True, stop=True)
                    last.then_inc(S("small_done"), 1)

                def token_rows(step):
                    n, p = step.n, step.p
                    v = rkv[p][:, 2, :, :, :].rearrange("p d h n -> p (d h) n")
                    for i, (src, b) in enumerate(((aT[p], 6), (v, 7), (bhT[p], 4), (khT[p], 5), (rT[p], 6))):
                        if i == 1:
                            pe.wait_ge(S("small_moved"), n + 1)
                            hold(pe, "pe")
                        if i == 2:
                            pe.wait_ge(S("raw_moved"), n + 1)
                            pe.wait_ge(S("ready"), n * 3 + 3)
                            hold(pe, "pe")
                        if i == 4:
                            pe.wait_ge(S("tok_moved"), n * 5 + 1)
                            hold(pe, "pe")
                        for dh in range(4):
                            last = nc.tensor.transpose(ps[:, b, dh * P:dh * P + P], src[:, dh, :], ident[:, :])
                        last.then_inc(S("tok_done"), 1)

                def groups_of(out, terms):
                    for e, dh, pz in SLOTS:
                        t = slice(C * pz, C * pz + C)
                        parts = terms(e, dh, pz, t)
                        for i, (a, b) in enumerate(parts):
                            last = mm(out[t, e, dh, :], a, b, start=(i == 0), stop=(i == len(parts) - 1))
                    return last

                def pairs_of(out, left, right, second=None):
                    for e in range(2):
                        if e and second:
                            pe.wait_ge(*second)
                            hold(pe, "pe")
                        for dh in range(4):
                            last = mm(out(e, dh), left[:, e, dh, :], right(e, dh), start=True, stop=True)
                    return last

                def main(step, nxt):
                    n = step.n
                    banks = lambda b: lambda e, dh: ps[:, b + e, dh * P:dh * P + P]
                    compact = lambda b: lambda e, dh: slots(b)[:, e, dh, :]
                    of = lambda t: lambda e, dh: t[:, e, dh, :]
                    of_tok = lambda t: lambda e, dh: t[:, dh, e, :]
                    products(step)
                    token_rows(step)
                    tok = lambda T, e, dh, t: T[t, dh, e, :]
                    pe.wait_ge(S("masked"), n * 2 + 2)
                    pe.wait_ge(S("tok_moved"), n * 5 + 2)
                    hold(pe, "pe")
                    groups_of(slots(3), lambda e, dh, pz, t: [(AkT[t, e, dh, :], tok(V_tok, e, dh, t))]).then_inc(S("z_done"), 1)
                    for j in range(5):
                        pe.wait_ge(S("lev_done"), n * 5 + (j + 1))
                        if j:
                            pe.wait_ge(S("xt_added"), n * 10 + (2 * j - 1))
                        hold(pe, "pe")
                        pairs_of(banks(0), lev[:, j, :, :, :], of(XT),
                                 (S("xt_added"), n * 10 + 2 * j) if j else None).then_inc(S("yt_done"), 1)
                        pe.wait_ge(S("yt_moved_a"), n * 5 + (j + 1))
                        pe.wait_ge(S("yt_moved_v"), n * 5 + (j + 1))
                        if j:
                            pe.wait_ge(S("x_added"), n * 4 + j)
                        else:
                            pe.wait_ge(S("x_made"), n + 1)
                            pe.wait_ge(S("z_moved"), n + 1)
                        hold(pe, "pe")
                        pairs_of(banks(2), X, of(YT)).then_inc(S("xt_done"), 1)
                        if j == 0:
                            pe.wait_ge(S("tok_moved"), n * 5 + 5)
                            hold(pe, "pe")
                        if j < 4:
                            pairs_of(banks(4), YT, of(X)).then_inc(S("xx_done"), 1)
                        if nxt and j == 0:
                            pe.wait_ge(S("tok_moved"), n * 5 + 5)
                            hold(pe, "pe")
                            lora_products(nxt)
                        if nxt and j == 2:
                            norm_sums(nxt)
                    pe.wait_ge(S("xt_added"), n * 10 + 9)
                    hold(pe, "pe")
                    pairs_of(compact(0), XT, of_tok(A_tok), (S("xt_added"), n * 10 + 10)).then_inc(S("pu_done"), 1)
                    pairs_of(compact(1), XT, of(Z)).then_inc(S("pu_done"), 1)
                    pe.wait_ge(S("p_moved_v"), n + 1)
                    pe.wait_ge(S("p_moved_a"), n + 1)
                    hold(pe, "pe")
                    pairs_of(compact(2), Pm, of_tok(B_tok)).then_inc(S("gq_done"), 1)
                    for e in range(2):
                        for dh in range(4):
                            mm(slots(3)[:, e, dh, :], Pm[:, e, dh, :], RbT[:, e, dh, :], start=True, stop=False)
                            last = mm(slots(3)[:, e, dh, :], R_wide[:, dh, e, :], masks[:, M_EYE, 0, :], start=False, stop=True)
                    last.then_inc(S("gq_done"), 1)
                    pe.wait_ge(S("u_moved"), n + 1)
                    pe.wait_ge(S("g_moved"), n + 1)
                    hold(pe, "pe")
                    if step.s == 0:
                        pe.wait_ge(S("zeroed"), 1)
                    else:
                        pe.wait_ge(S("state_in"), 32)
                    for rnd in range(2):
                        if rnd:
                            pe.wait_ge(S("m_moved_v"), n * 2 + 1)
                            pe.wait_ge(S("m_moved_a"), n * 2 + 1)
                            hold(pe, "pe")
                        mine = [(e, dh, rnd if dh < 2 else 1 - rnd) for e in range(2) for dh in range(4)]
                        for e, dh, pz in mine:
                            t, o = slice(C * pz, C * pz + C), slice(C * (1 - pz), C * (1 - pz) + C)
                            for i, (a, b) in enumerate(((tok(B_tok, e, dh, t), U[t, e, dh, :]), (tok(K_tok, e, dh, t), tok(V_tok, e, dh, t)),
                                                        (GT[t, e, dh, :], M[t, e, dh, :]))):
                                last = mm(slots(5)[o, e, dh, :], a, b, start=(i == 0), stop=(i == 2))
                        last.then_inc(S("m_done"), 1)
                        if rnd == 0:
                            pe.wait_ge(S("q_moved"), n + 1)
                            hold(pe, "pe")
                        for e, dh, pz in mine:
                            t = slice(C * pz, C * pz + C)
                            for i, (a, b) in enumerate(((RbT[t, e, dh, :], U[t, e, dh, :]), (RkT[t, e, dh, :], tok(V_tok, e, dh, t)),
                                                        (QT[t, e, dh, :], M[t, e, dh, :]))):
                                last = mm(slots(4)[t, e, dh, :], a, b, start=(i == 0), stop=(i == 2))
                    last.then_inc(S("y_done"), 1)

                pe.wait_ge(S("const_in"), 16 * n_const)
                first = Step(0, 0, None, None)
                lora_products(first)
                norm_sums(first)
                over_steps(pe, main)


def phase_scan_output(core, l):
    nc, d, hold = core.nc, core.dram, core.hold
    with ExitStack() as mem:
        def sb(name, shape):
            return mem.enter_context(nc.sbuf_tensor(name, shape, F32))
        o = sb("o_sum", [P, NT, D_RWKV])
        other = sb("o_other", [P, NT, D_RWKV])
        bonus = sb("o_bonus", [P, NT, D_RWKV])
        bonus2 = sb("o_bonus2", [P, NT, D_RWKV])
        ln = sb("o_ln", [P, 2, D_RWKV])
        mean = sb("o_mean", [P, NT * N_RWKV])
        var = sb("o_var", [P, NT * N_RWKV])
        eps = sb("o_eps", [P, 1])
        loaded, bonus_in, out_done, sent, bonus_done, eps_done, var_done, root_done = (
            core.sem(f"o_{n}") for n in ("loaded", "bonus_in", "out_done", "sent", "bonus_done", "eps_done", "var_done", "root_done"))
        flat = lambda t: t[:, :, :].rearrange("p t c -> p (t c)")
        heads = lambda t: t[:, :, :].rearrange("p t (h c) -> p (t h) c", c=HD)
        with nc.Block() as block:
            @block.sync
            def _(sp):
                for i, t in enumerate((o, other)):
                    sp.dma_start(t[:, :, :], d["scan_tok"][i * TOK:(i + 1) * TOK, :].rearrange("(t p) c -> p t c", p=P)).then_inc(loaded, 16)
                sp.dma_start(ln[:, :, :], d["rwkv_ln"][bass.ds(l, 1), :, :].rearrange("a i c -> a (i c)").broadcast_to([P, 2 * D_RWKV])
                             .rearrange("p (i c) -> p i c", i=2)).then_inc(loaded, 16)
                sp.wait_ge(out_done, 1)
                sp.dma_start(d["mix_tok"][:, 0:D_RWKV].rearrange("(t p) c -> p t c", p=P), o[:, :, :]).then_inc(sent, 16)
                sp.wait_ge(sent, 16)

            @block.gpsimd
            def _(pool):
                pool.wait_ge(bonus_in, 32)
                nc.gpsimd.tensor_tensor(flat(bonus), flat(bonus), flat(bonus2), ALU.add)
                pool.drain()
                pool.wait_ge(loaded, 48)
                nc.gpsimd.tensor_tensor(bonus[:, :, :], bonus[:, :, :], ln[:, 1, :].unsqueeze(1).broadcast_to([P, NT, D_RWKV]),
                                        ALU.add).then_inc(bonus_done, 1)

            @block.scalar
            def _(act):
                for i, t in enumerate((bonus, bonus2)):
                    act.dma_start(t[:, :, :], d["bonus_tok"][i * TOK:(i + 1) * TOK, :].rearrange("(t p) c -> p t c", p=P)).then_inc(bonus_in, 16)
                act.wait_ge(eps_done, 1)
                act.wait_ge(var_done, 1)
                nc.scalar.activation(var[:, :], var[:, :], ACT.Sqrt, scale=1.0 / HD, bias=eps[:, :]).then_inc(root_done, 1)

            @block.vector
            def _(dve):
                G = NT * N_RWKV
                tt = nc.vector.tensor_tensor
                nc.vector.memset(eps[:, :], GN_EPS).then_inc(eps_done, 1)
                dve.wait_ge(loaded, 48)
                tt(flat(o), flat(o), flat(other), ALU.add)
                dve.drain()
                nc.vector.tensor_reduce(mean[:, :], heads(o), AX, ALU.add)
                dve.drain()
                nc.vector.tensor_scalar(mean[:, :], mean[:, :], 1.0 / HD, None, ALU.mult)
                dve.drain()
                tt(heads(o), heads(o), mean[:, :].unsqueeze(2).broadcast_to([P, G, HD]), ALU.subtract)
                dve.drain()
                tt(flat(other), flat(o), flat(o), ALU.mult)
                dve.drain()
                nc.vector.tensor_reduce(var[:, :], heads(other), AX, ALU.add).then_inc(var_done, 1)
                tt(o[:, :, :], o[:, :, :], ln[:, 0, :].unsqueeze(1).broadcast_to([P, NT, D_RWKV]), ALU.mult)
                dve.wait_ge(root_done, 1)
                nc.vector.reciprocal(mean[:, :], var[:, :])
                dve.drain()
                tt(heads(o), heads(o), mean[:, :].unsqueeze(2).broadcast_to([P, G, HD]), ALU.mult)
                dve.wait_ge(bonus_done, 1)
                dve.drain()
                tt(flat(o), flat(o), flat(bonus), ALU.add).then_inc(out_done, 1)


V_W = HD + 1
NA_LOCAL = (NA_ROWS + 1) * GRID
NA_KEYS = NA_LOCAL + PAST
NQ = LAT // P
OWN_COL = PAST + LAT
OWN_TILE = OWN_COL // P
UNITS = 6


class Query:

    def __init__(self, t, n, row, first=None, edge=None):
        self.t, self.n, self.row, self.first, self.edge, self.p = t, n, row, first, edge, t % 2


def over_queries(eng, body):
    def make(t):
        edge = t < 2 or t >= NQ - 2
        rs = 0 if t < 2 else 2 * (NQ - 4)
        return Query(t, t, CTX + t * P, *((rs // 2, rs - 2 * t + NA_ROWS - 1) if edge else (t - 2, None)))
    for t in (0, 2):
        body([make(t), make(t + 1)], make(t - 1) if t else None)
    with eng.Fori(0, NQ // 2 - 3) as j:
        looped = [Query(3 + o, j * 2 + (3 + o), j * (2 * P) + CTX + (3 + o) * P, j * 2 + (1 + o)) for o in range(3)]
        body(looped[1:], looped[0])
    body([make(NQ - 2), make(NQ - 1)], make(NQ - 3))
    return make(NQ - 1)


class Attention:

    def __init__(self, core, mem, name, score_banks, keys, n_exp):
        nc = core.nc
        self.core, self.nc, self.n_exp = core, nc, n_exp
        self.groups = -(-(-(-keys // P)) // 4)
        self.per = ((self.groups + 1) // 2, self.groups // 2)
        self.probsT_done = [core.sem(f"{name}_probsT{i}_done") for i in range(2)]
        self.ident = mem.enter_context(nc.sbuf_tensor(f"{name}_ident", [P, P], F32))
        self.probs = mem.enter_context(nc.sbuf_tensor(f"{name}_probs", [P, 2, keys], F32))
        self.probsT = mem.enter_context(nc.sbuf_tensor(f"{name}_probsT", [P, -(-keys // P), P], F32))
        self.stat = mem.enter_context(nc.sbuf_tensor(f"{name}_stat", [P, 4], F32))
        self.rsum = mem.enter_context(nc.sbuf_tensor(f"{name}_rsum", [P, UNITS], F32))
        self.out = mem.enter_context(nc.sbuf_tensor(f"{name}_out", [P, 2, UNITS, HD], F32))
        self.ps_s = mem.enter_context(nc.psum_tensor(f"{name}_ps_s", [P, score_banks * CHUNK], F32))
        self.ps_t = [mem.enter_context(nc.psum_tensor(f"{name}_ps_t{i}", [P, 4, P], F32)) for i in range(2)]
        self.ps_o = mem.enter_context(nc.psum_tensor(f"{name}_ps_o", [P, UNITS, V_W], F32))
        self.q_in = [core.sem(f"{name}_q{p}_in") for p in range(2)]
        self.out_sent = [core.sem(f"{name}_out{p}_sent") for p in range(2)]
        (self.score_done, self.max_done, self.exp_done, self.turn_done, self.value_done, self.out_done) = (
            core.sem(f"{name}_{n}") for n in
            ("score_done", "max_done", "exp_done", "turn_done", "value_done", "out_done"))

    def turn_and_multiply(self, pe, u, first, tiles, groups, v_of):
        hold = self.core.hold
        h = u.h
        turns = [tiles[4 * g:4 * g + 4] for g in range(groups)]

        def turn(g):
            if g == 0:
                pe.wait_ge(self.exp_done, u.n * self.n_exp + self.n_exp)
                hold(pe, "pe")
            if g >= 2 or not first:
                pe.wait_ge(self.probsT_done[g % 2], u.n * self.per[g % 2] + g // 2)
                hold(pe, "pe")
            for i, (lo, width) in enumerate(turns[g]):
                tr = self.nc.tensor.transpose(self.ps_t[g % 2][0:width, i, :], self.probs[:, u.p, lo:lo + width], self.ident[:, :])
            tr.then_inc(self.turn_done, 1)

        def multiply(g):
            pe.wait_ge(self.probsT_done[g % 2], u.n * self.per[g % 2] + (g // 2 + 1))
            hold(pe, "pe")
            if g == 0 and h == 0 and not first:
                pe.wait_ge(self.out_done, u.q.n)
                hold(pe, "pe")
            for i, (lo, width) in enumerate(turns[g]):
                k = 4 * g + i
                mm = self.nc.tensor.matmul(self.ps_o[:, h, :], self.probsT[0:width, k, :], v_of(k),
                                           start=(k == 0), stop=(k == len(tiles) - 1))
            if g == groups - 1:
                mm.then_inc(self.value_done, 1)

        turn(0)
        for g in range(1, groups):
            turn(g)
            multiply(g - 1)
        multiply(groups - 1)

    def to_sbuf(self, eng, who, copy, u, g, groups, tiles):
        eng.wait_ge(self.turn_done, u.n * groups + (g + 1))
        self.core.hold(eng, who)
        blocks = tiles[4 * g:4 * g + 4]
        runs = []
        for i, (lo, width) in enumerate(blocks):
            if runs and runs[-1][2] == width:
                runs[-1][1] = i + 1
            else:
                runs.append([i, i + 1, width])
        for a, b, width in runs:
            last = copy(self.probsT[0:width, 4 * g + a:4 * g + b, :], self.ps_t[g % 2][0:width, a:b, :])
        last.then_inc(self.probsT_done[g % 2], 1)

    def normalise(self, dve, q):
        hold = self.core.hold
        dve.wait_ge(self.value_done, q.n * UNITS + UNITS)
        hold(dve, "dve")
        self.nc.vector.reciprocal(self.rsum[:, :], self.ps_o[:, :, HD])
        if q.t > 1:
            dve.wait_ge(self.out_sent[q.p], same_parity(q, 16))
            hold(dve, "dve")
        dve.drain()
        self.nc.vector.tensor_tensor(self.out[:, q.p, :, :], self.ps_o[:, :, 0:HD],
                                     self.rsum[:, :].unsqueeze(2).broadcast_to([P, UNITS, HD]), ALU.mult).then_inc(self.out_done, 1)


class Unit:

    def __init__(self, q, h):
        self.q, self.h, self.n, self.p = q, h, q.n * UNITS + h, h % 2
        self.first = q.t == 0 and h == 0


def units_of(pair, before):
    units = ([Unit(before, UNITS - 1)] if before else [None]) + [Unit(q, h) for q in pair for h in range(UNITS)]
    return list(zip(units[1:], units))


def same_parity(q, each):
    return (q.n - q.p) * (each // 2)


def phase_neighbourhood(core, l):
    nc, d, hold = core.nc, core.dram, core.hold
    N_DR = 2 * NA_ROWS - 1
    tiles_in = [(i * P, P) for i in range(4)] + [(4 * P, GRID)] + [(NA_LOCAL + i * P, P) for i in range(2)]
    tiles_edge = [(i * P, P) for i in range(6)]
    groups = 2
    with ExitStack() as mem:
        def sb(name, shape):
            return mem.enter_context(nc.sbuf_tensor(name, shape, F32))
        kT = sb("n_kT", [P, N_NA // 2, LAT])
        kT_ctx = sb("n_kT_ctx", [P, N_NA // 2, PAST])
        v = sb("n_v", [P, NQ, N_NA, V_W])
        v_ctx = sb("n_v_ctx", [P, 2, N_NA, V_W])
        qT = sb("n_qT", [P, 2, N_NA // 2, 2, P])
        windows = sb("n_windows", [GRID, N_NA * N_DR, GRID])
        flip = sb("n_flip", [GRID, P])
        col_mask = sb("n_col_mask", [P, GRID])
        bias = sb("n_bias", [P, N_NA, N_DR + 1, GRID])
        bias_in = sb("n_bias_in", [P, N_NA, NA_LOCAL])
        scores = sb("n_scores", [P, 2, NA_KEYS])
        at = Attention(core, mem, "n", 2, NA_KEYS, 1)
        ps_b = [mem.enter_context(nc.psum_tensor(f"n_ps_b{i}", [P, CHUNK // GRID, GRID], F32)) for i in range(2)]
        const_in, ones_done, bias_mm, bias_half, table_done = (core.sem(f"n_{n}") for n in
                                                              ("const_in", "ones_done", "bias_mm", "bias_half", "table_done"))
        score_read = core.sem("n_score_read")
        parts = [(h, a, b) for h in range(N_NA) for a, b in ((0, 8), (8, N_DR))]

        with nc.Block() as block:
            @block.sync
            def _(sp):
                sp.wait_ge(ones_done, 3)
                sp.dma_start(at.ident[:, :], d["ident"]).then_inc(const_in, 16)
                sp.dma_start(flip[:, :], d["flip"]).then_inc(const_in, 16)
                sp.dma_start(col_mask[:, :], d["col_mask"]).then_inc(const_in, 16)
                rows = d["rpb_pad"][bass.ds(l * (N_NA * N_DR), N_NA * N_DR), :]
                sp.dma_start(windows[:, :, :], bass.AP(rows.tensor, rows.offset, [[1, GRID], [P, N_NA * N_DR], [1, GRID]])).then_inc(const_in, 16)
                sp.dma_start(kT_ctx[:, :, :], d["na_kT"][bass.ds(l * D_NA, D_NA), :].rearrange("(h p) n -> p h n", p=P)).then_inc(const_in, 16)
                kn = d["feat_attn"][D_NA:2 * D_NA, CTX:TOK].rearrange("(h p) n -> p h n", p=P)
                for a, b in ((0, 2), (2, 3)):
                    sp.dma_start(kT[:, a:b, :], kn[:, a:b, :]).then_inc(const_in, 16)
                with nc.allow_non_contiguous_dma(reason="rows of one head"):
                    for i in range(2):
                        sp.dma_start(v_ctx[:, i, :, 0:HD], d["na_v"][bass.ds(l * PAST + i * P, P), :]
                                     .rearrange("p (h e) -> p h e", e=HD)).then_inc(const_in, 16)
                    for t in range(NQ):
                        sp.dma_start(v[:, t, :, 0:HD], d["vn_tok"][CTX + t * P:CTX + (t + 1) * P, :]
                                     .rearrange("p (h e) -> p h e", e=HD)).then_inc(const_in, 16)

                def body(pair, before):
                    for q in pair:
                        if q.t > 1:
                            sp.wait_ge(at.score_done, q.n * UNITS - UNITS)
                            hold(sp, "sp")
                        qn = d["feat_attn"][0:D_NA, bass.ds(q.row, P)].rearrange("(h p) n -> p h n", p=P)
                        for e in range(2):
                            rows = slice(HD * e, HD * e + HD)
                            sp.dma_start(qT[rows, q.p, :, e, :], qn[rows, :, :]).then_inc(at.q_in[q.p], 16)
                over_queries(sp, body)

            @block.gpsimd
            def _(pool):
                nc.gpsimd.memset(v[:, :, :, :], 1.0).then_inc(ones_done, 1)
                nc.gpsimd.memset(v_ctx[:, :, :, :], 1.0).then_inc(ones_done, 1)
                nc.gpsimd.memset(qT[:, :, :, :, :], 0.0).then_inc(ones_done, 1)
                pool.wait_ge(bias_half, 2 * len(parts))
                bi = bias_in[:, :, :].rearrange("p h (m c) -> p h m c", c=GRID)
                nc.gpsimd.tensor_copy(bi[0:GRID, :, 0:8, :], bias[0:GRID, :, 3:11, :])
                nc.gpsimd.tensor_copy(bi[GRID:P, :, 1:9, :], bias[GRID:P, :, 4:12, :])
                nc.gpsimd.memset(bi[0:GRID, :, 8, :], NEG)
                nc.gpsimd.memset(bi[GRID:P, :, 0, :], NEG).then_inc(table_done, 1)

                def body(pair, before):
                    for q in pair:
                        pool.wait_ge(at.out_done, q.n + 1)
                        hold(pool, "pool")
                        pool.dma_start(d["mix_tok"][bass.ds(q.row, P), D_RWKV:D_RWKV + D_NA], at.out[:, q.p, :, :]
                                       .rearrange("p h e -> p (h e)")).then_inc(at.out_sent[q.p], 16)
                over_queries(pool, body)
                for p in range(2):
                    pool.wait_ge(at.out_sent[p], 8 * NQ)

            @block.scalar
            def _(act):
                def exp(u):
                    act.wait_ge(at.max_done, u.n + 1)
                    hold(act, "act")
                    keys = NA_KEYS if u.q.edge is None else NA_KEYS - GRID
                    nc.scalar.activation(at.probs[:, u.p, 0:keys], scores[:, u.p, 0:keys], ACT.Exp,
                                         bias=at.stat[:, u.p:u.p + 1]).then_inc(at.exp_done, 1)

                def move(u):
                    tiles = tiles_in if u.q.edge is None else tiles_edge
                    for g in range(groups):
                        at.to_sbuf(act, "act", lambda o, i: nc.scalar.activation(o, i, ACT.Copy), u, g, groups, tiles)

                def body(pair, before):
                    for u, last in units_of(pair, before):
                        if last:
                            move(last)
                        exp(u)
                move(Unit(over_queries(act, body), UNITS - 1))

            @block.vector
            def _(dve):
                dve.wait_ge(const_in, 16 * (9 + NQ))
                for i, (h, a, b) in enumerate(parts):
                    dve.wait_ge(bias_mm, i + 1)
                    for e in range(2):
                        rows = slice(GRID * e, GRID * e + GRID)
                        nc.vector.tensor_tensor(bias[rows, h, a + e:b + e, :], ps_b[i % 2][rows, 0:b - a, :],
                                                col_mask[rows, :].unsqueeze(1).broadcast_to([GRID, b - a, GRID]),
                                                ALU.add).then_inc(bias_half, 1)
                dve.wait_ge(table_done, 1)

                def maximum(u):
                    dve.wait_ge(at.score_done, u.n + 1)
                    hold(dve, "dve")
                    if u.q.t > 0 or u.h > 1:
                        dve.wait_ge(at.exp_done, u.n - 1)
                        hold(dve, "dve")
                    edge = u.q.edge
                    local = NA_LOCAL if edge is None else NA_LOCAL - GRID
                    keys = local + PAST
                    table = bias_in[:, u.h, :] if edge is None else bias[:, u.h, edge:edge + 8, :].rearrange("p m c -> p (m c)")
                    nc.vector.tensor_tensor(scores[:, u.p, 0:local], at.ps_s[:, 0:local], table, ALU.add)
                    nc.vector.tensor_copy(scores[:, u.p, local:keys], at.ps_s[:, local:keys]).then_inc(score_read, 1)
                    dve.drain()
                    nc.vector.tensor_reduce(at.stat[:, u.p:u.p + 1], scores[:, u.p, 0:keys], AX, ALU.max, negate=True)\
                        .then_inc(at.max_done, 1)

                def body(pair, before):
                    for u, last in units_of(pair, before):
                        maximum(u)
                        if last and u.h == 0:
                            at.normalise(dve, last.q)
                at.normalise(dve, over_queries(dve, body))

            @block.tensor
            def _(pe):
                pe.wait_ge(const_in, 16 * (9 + NQ))
                for i, (h, a, b) in enumerate(parts):
                    if i >= 2:
                        pe.wait_ge(bias_half, 2 * (i - 1))
                    nc.tensor.matmul(ps_b[i % 2][:, 0:b - a, :], flip[:, :], windows[:, h * N_DR + a:h * N_DR + b, :],
                                     start=True, stop=True).then_inc(bias_mm, 1)

                def score(u):
                    q = u.q
                    if u.h == 0:
                        pe.wait_ge(at.q_in[q.p], same_parity(q, 32) + 32)
                        hold(pe, "pe")
                    if not u.first:
                        pe.wait_ge(score_read, u.n)
                        hold(pe, "pe")
                    lhs = qT[:, q.p, u.h // 2, u.h % 2, :]
                    blocks = 9 if q.edge is None else 8
                    key = q.first * P
                    nc.tensor.matmul(at.ps_s[:, 0:CHUNK], lhs, kT[:, u.h // 2, bass.ds(key, CHUNK)], start=True, stop=True)
                    if blocks == 9:
                        nc.tensor.matmul(at.ps_s[:, CHUNK:NA_LOCAL], lhs, kT[:, u.h // 2, bass.ds(key + CHUNK, GRID)], start=True, stop=True)
                    nc.tensor.matmul(at.ps_s[:, blocks * GRID:blocks * GRID + PAST], lhs, kT_ctx[:, u.h // 2, :],
                                     start=True, stop=True).then_inc(at.score_done, 1)

                def values(u):
                    q = u.q
                    n_local = 5 if q.edge is None else 4
                    tiles = tiles_in if q.edge is None else tiles_edge

                    def v_of(k):
                        if k >= n_local:
                            return v_ctx[:, k - n_local, u.h, :]
                        width = tiles[k][1]
                        return v[0:width, bass.ds(q.first + k, 1), u.h, :].rearrange("p a e -> p (a e)")
                    at.turn_and_multiply(pe, u, u.first, tiles, groups, v_of)

                def body(pair, before):
                    for u, last in units_of(pair, before):
                        score(u)
                        if last:
                            values(last)
                values(Unit(over_queries(pe, body), UNITS - 1))


class KeyTile:

    def __init__(self, j, n, row, dst, h):
        self.j, self.n, self.row, self.dst, self.h, self.p = j, n, row, dst, h, j % 2
        self.past, self.has_q = j < 2, j >= 2


NKT = 2 + NT


def over_key_tiles(eng, body):
    def make(j):
        return KeyTile(j, j, (j - 2) * P, j if j < 2 else OWN_TILE if j == 2 else j - 1, j // 2)
    fixed = [make(j) for j in range(5)]
    for a, b in zip([None] + fixed, fixed):
        body(b, a)
    with eng.Fori(0, (NKT - 5) // 2) as i:
        looped = [KeyTile(j, i * 2 + j, i * (2 * P) + (j - 2) * P, i * 2 + (j - 1), i + j // 2) for j in (4, 5, 6)]
        for a, b in zip(looped, looped[1:]):
            body(b, a)
    return make(NKT - 1)


class LatentKeys:

    def __init__(self, core, mem):
        sb = lambda name, shape: mem.enter_context(core.nc.sbuf_tensor(name, shape, F32))
        self.kT = sb("l_kT_all", [MLA_D, N_MLA, PAST + TOK])
        self.v = sb("l_v_all", [P, OWN_TILE + 1, N_MLA, V_W])


def phase_latent_keys(core, l, keys):
    nc, d, hold = core.nc, core.dram, core.hold
    H = N_MLA
    QW = H * MLA_D
    HALF = ROPE // 2
    with ExitStack() as mem:
        def sb(name, shape):
            return mem.enter_context(nc.sbuf_tensor(name, shape, F32))
        ident = sb("k_ident", [P, P])
        eps = sb("k_eps", [P, 1])
        w_uk = sb("k_w_uk", [P, D_MLA])
        w_uv = sb("k_w_uv", [P, D_MLA])
        w_uq = sb("k_w_uq", [P, 2, QW])
        norm_wt = sb("k_norm_wt", [P, 2, MLA_D])
        ckvT = sb("k_ckvT", [P, 2, P])
        cqT = sb("k_cqT", [P, 2, 2, P])
        krope = sb("k_krope", [P, 2, ROPE])
        rope = sb("k_rope", [P, 2, ROPE])
        sq = sb("k_sq", [P, D_MLA + QW])
        sums = sb("k_sums", [P, 3, 13])
        k_tok = sb("k_k_tok", [P, 2, H, MLA_D])
        q_tok = sb("k_q_tok", [P, 2, H, MLA_D])
        krope_sq = sb("k_krope_sq", [P, ROPE])
        kr = sb("k_kr", [P, 4, HALF])
        kro = sb("k_kro", [P, ROPE])
        qr = sb("k_qr", [P, 4, H, HALF])
        qT = sb("k_qT", [MLA_D, 2, H, P])
        ps_k = mem.enter_context(nc.psum_tensor("k_ps_k", [P, CHUNK], F32))
        ps_v = mem.enter_context(nc.psum_tensor("k_ps_v", [P, CHUNK], F32))
        ps_q = mem.enter_context(nc.psum_tensor("k_ps_q", [P, 2 * CHUNK], F32))
        ps_kT = mem.enter_context(nc.psum_tensor("k_ps_kT", [P, 8, P], F32))
        ps_qT = mem.enter_context(nc.psum_tensor("k_ps_qT", [P, 8, P], F32))
        const_in, ready = core.sem("k_const_in"), core.sem("k_ready")
        tile_in = [core.sem(f"k_tile{p}_in") for p in range(2)]
        qT_out = [core.sem(f"k_qT{p}_out") for p in range(2)]
        product, sq_done, sum_done, root_done, v_done, norm_done, turn_done, moved = (
            core.sem(f"k_{n}") for n in ("product", "sq_done", "sum_done", "root_done", "v_done", "norm_done", "turn_done", "moved"))
        used = core.sem("k_used")
        each = 4 * 16

        def in_before(t):
            return t.h * each

        def q_before(t):
            return (t.h - 1) * 16

        with nc.Block() as block:
            @block.sync
            def _(sp):
                sp.dma_start(ident[:, :], d["ident"]).then_inc(const_in, 16)
                for name, to in (("w_uk", w_uk), ("w_uv", w_uv)):
                    sp.dma_start(to[:, :], d[name][bass.ds(l, 1), :, :].rearrange("a p n -> (a p) n")).then_inc(const_in, 16)
                sp.dma_start(w_uq[:, :, :], d["w_uq"][bass.ds(l, 1), :, :].rearrange("a (k p) n -> p (a k) n", p=P)).then_inc(const_in, 16)
                for i, name in enumerate(("q_norm", "k_norm")):
                    sp.dma_start(norm_wt[:, i, :], d["mla_" + name][bass.ds(l, 1), :].broadcast_to([P, MLA_D])).then_inc(const_in, 16)

                def body(t, prev):
                    if t.j > 1:
                        sp.wait_ge(norm_done, t.n - 1)
                        hold(sp, "sp")
                    row = 0 if t.past else t.row
                    if t.past:
                        sp.dma_start(ckvT[:, t.p, :], d["past_ckvT"][bass.ds(l, 1), :, t.j * P:(t.j + 1) * P]
                                     .rearrange("a p n -> (a p) n")).then_inc(tile_in[t.p], 16)
                        sp.dma_start(krope[:, t.p, :], d["past_krope"][bass.ds(l * PAST + t.j * P, P), :]).then_inc(tile_in[t.p], 16)
                    else:
                        sp.dma_start(ckvT[:, t.p, :], d["feat_attn"][8 * P:9 * P, bass.ds(row, P)]).then_inc(tile_in[t.p], 16)
                        sp.dma_start(krope[:, t.p, :], d["krope_tok"][bass.ds(row, P), :]).then_inc(tile_in[t.p], 16)
                    sp.dma_start(rope[:, t.p, :], d["rope"][bass.ds(row, P), :]).then_inc(tile_in[t.p], 16)
                    sp.dma_start(cqT[:, t.p, :, :], d["feat_attn"][6 * P:8 * P, bass.ds(row, P)]
                                 .rearrange("(k p) n -> p k n", p=P)).then_inc(tile_in[t.p], 16)
                over_key_tiles(sp, body)

            @block.gpsimd
            def _(pool):
                nc.gpsimd.memset(keys.v[:, :, :, :], 1.0)
                nc.gpsimd.memset(eps[:, :], EPS).then_inc(ready, 1)

                def store(t):
                    if t.has_q:
                        pool.wait_ge(moved, t.n * 2 + 2)
                        hold(pool, "pool")
                        pool.dma_start(d["mla_q"].rearrange("(h e) n -> e h n", e=MLA_D)[:, :, bass.ds(t.row, P)],
                                       qT[:, t.p, :, :]).then_inc(qT_out[t.p], 16)

                def body(t, prev):
                    if prev:
                        store(prev)
                store(over_key_tiles(pool, body))
                pool.wait_ge(qT_out[0], 16 * 9)
                pool.wait_ge(qT_out[1], 16 * 8)

            @block.scalar
            def _(act):
                def squares(t):
                    act.wait_ge(product, t.n + 1)
                    hold(act, "act")
                    if t.j > 0:
                        act.wait_ge(norm_done, t.n)
                        hold(act, "act")
                    nc.scalar.activation(sq[:, 0:D_MLA], ps_k[:, 0:D_MLA], ACT.Square)
                    nc.scalar.activation(sq[:, D_MLA:], ps_q[:, 0:QW], ACT.Square).then_inc(sq_done, 1)
                    nc.scalar.activation(krope_sq[:, :], krope[:, t.p, :], ACT.Square, accum_out=sums[:, 0, 12:13]).then_inc(sq_done, 1)
                    nc.scalar.activation(keys.v[:, bass.ds(t.dst, 1), :, 0:HD].rearrange("p a h e -> p (a h) e"),
                                         ps_v[:, 0:D_MLA].rearrange("p (h e) -> p h e", e=HD), ACT.Copy).then_inc(v_done, 1)
                    act.wait_ge(sum_done, t.n + 1)
                    hold(act, "act")
                    nc.scalar.activation(sums[:, 1, 0:12], sums[:, 0, 0:12], ACT.Sqrt, scale=1.0 / MLA_D, bias=eps[:, :]).then_inc(root_done, 1)

                def move(t):
                    act.wait_ge(turn_done, t.n + 1)
                    hold(act, "act")
                    nc.scalar.activation(keys.kT[:, :, bass.ds(t.dst * P, P)], ps_kT[0:MLA_D, 0:H, :], ACT.Copy).then_inc(moved, 1)
                    if t.j > 3:
                        act.wait_ge(qT_out[t.p], q_before(t))
                        hold(act, "act")
                    nc.scalar.activation(qT[:, t.p, :, :], ps_qT[0:MLA_D, 0:H, :], ACT.Copy).then_inc(moved, 1)

                def body(t, prev):
                    squares(t)
                    if prev:
                        move(prev)
                act.wait_ge(ready, 1)
                act.wait_ge(const_in, 16 * 6)
                move(over_key_tiles(act, body))

            @block.vector
            def _(dve):
                def rotate(x1, x2, o1, o2, tmp, cos, sin):
                    for i, (a, b) in enumerate(((x1, cos), (x2, sin), (x2, cos), (x1, sin))):
                        nc.vector.tensor_tensor(tmp[i], a, b, ALU.mult)
                    dve.drain()
                    nc.vector.tensor_tensor(o1, tmp[0], tmp[1], ALU.subtract)
                    nc.vector.tensor_tensor(o2, tmp[2], tmp[3], ALU.add)

                def norms(t):
                    dve.wait_ge(sq_done, t.n * 2 + 2)
                    hold(dve, "dve")
                    nc.vector.tensor_reduce(sums[:, 0, 0:6], sq[:, 0:D_MLA].rearrange("p (h e) -> p h e", e=HD), AX, ALU.add)
                    nc.vector.tensor_reduce(sums[:, 0, 6:12], sq[:, D_MLA:].rearrange("p (h e) -> p h e", e=MLA_D), AX, ALU.add)
                    dve.drain()
                    nc.vector.tensor_scalar(sums[:, 0, 0:6], sums[:, 0, 0:6], sums[:, 0, 12:13], None, ALU.add).then_inc(sum_done, 1)
                    nc.vector.tensor_tensor(kro[:, :], krope[:, t.p, :], norm_wt[:, 1, HD:MLA_D], ALU.mult)
                    dve.drain()
                    cos, sin = rope[:, t.p, 0:HALF], rope[:, t.p, HALF:ROPE]
                    rotate(kro[:, 0:HALF], kro[:, HALF:ROPE], kro[:, 0:HALF], kro[:, HALF:ROPE],
                           [kr[:, i, :] for i in range(4)], cos, sin)
                    dve.wait_ge(root_done, t.n + 1)
                    hold(dve, "dve")
                    nc.vector.reciprocal(sums[:, 2, 0:12], sums[:, 1, 0:12])
                    if t.j > 1:
                        dve.wait_ge(turn_done, t.n - 1)
                        hold(dve, "dve")
                    dve.drain()
                    rk = sums[:, 2, 0:6].unsqueeze(2)
                    rq = sums[:, 2, 6:12].unsqueeze(2)
                    kt, qt = k_tok[:, t.p, :, :], q_tok[:, t.p, :, :]
                    nc.vector.tensor_tensor(kt[:, :, 0:HD], ps_k[:, 0:D_MLA].rearrange("p (h e) -> p h e", e=HD),
                                            rk.broadcast_to([P, H, HD]), ALU.mult)
                    nc.vector.tensor_tensor(kt[:, :, HD:MLA_D], kro[:, :].unsqueeze(1).broadcast_to([P, H, ROPE]),
                                            rk.broadcast_to([P, H, ROPE]), ALU.mult)
                    nc.vector.tensor_tensor(qt, ps_q[:, 0:QW].rearrange("p (h e) -> p h e", e=MLA_D),
                                            rq.broadcast_to([P, H, MLA_D]), ALU.mult).then_inc(used, 1)
                    dve.drain()
                    nc.vector.tensor_tensor(kt[:, :, 0:HD], kt[:, :, 0:HD], norm_wt[:, 1, 0:HD].unsqueeze(1).broadcast_to([P, H, HD]), ALU.mult)
                    nc.vector.tensor_tensor(qt, qt, norm_wt[:, 0, :].unsqueeze(1).broadcast_to([P, H, MLA_D]), ALU.mult)
                    dve.drain()
                    x1, x2 = qt[:, :, HD:HD + HALF], qt[:, :, HD + HALF:MLA_D]
                    rotate(x1, x2, x1, x2, [qr[:, i, :, :] for i in range(4)], cos.unsqueeze(1).broadcast_to([P, H, HALF]),
                           sin.unsqueeze(1).broadcast_to([P, H, HALF]))
                    dve.drain().then_inc(norm_done, 1)

                dve.wait_ge(const_in, 16 * 6)
                nc.vector.tensor_scalar(norm_wt[:, 0, :], norm_wt[:, 0, :], MLA_SCALE, None, ALU.mult)
                dve.drain()
                over_key_tiles(dve, lambda t, prev: norms(t))

            @block.tensor
            def _(pe):
                def products(t):
                    pe.wait_ge(tile_in[t.p], in_before(t) + each)
                    hold(pe, "pe")
                    if t.j > 0:
                        pe.wait_ge(used, t.n)
                        pe.wait_ge(v_done, t.n)
                        hold(pe, "pe")
                    nc.tensor.matmul(ps_k[:, 0:D_MLA], ckvT[:, t.p, :], w_uk[:, :], start=True, stop=True)
                    nc.tensor.matmul(ps_v[:, 0:D_MLA], ckvT[:, t.p, :], w_uv[:, :], start=True, stop=True)
                    for a, b in ((0, CHUNK), (CHUNK, QW)):
                        for k in range(2):
                            mm = nc.tensor.matmul(ps_q[:, a:b], cqT[:, t.p, k, :], w_uq[:, k, a:b], start=(k == 0), stop=(k == 1))
                    mm.then_inc(product, 1)

                def turns(t):
                    pe.wait_ge(norm_done, t.n + 1)
                    hold(pe, "pe")
                    if t.j > 0:
                        pe.wait_ge(moved, t.n * 2)
                        hold(pe, "pe")
                    for src, dst in ((k_tok, ps_kT), (q_tok, ps_qT)):
                        for h in range(H):
                            tr = nc.tensor.transpose(dst[0:MLA_D, h, :], src[:, t.p, h, :], ident[:, :])
                    tr.then_inc(turn_done, 1)

                def body(t, prev):
                    products(t)
                    if prev:
                        turns(prev)
                pe.wait_ge(const_in, 16 * 6)
                turns(over_key_tiles(pe, body))


def phase_latent_attention(core, l, keys):
    nc, d, hold = core.nc, core.dram, core.hold
    n_keys = PAST + LAT
    tiles = [(i * P, P) for i in range(n_keys // P)]
    groups = -(-len(tiles) // 4)
    chunks = [(c, min(c + CHUNK, n_keys)) for c in range(0, n_keys, CHUNK)]
    pieces = [(0, 1024), (1024, 2048), (2048, n_keys)]
    halves = [(0, 1536), (1536, n_keys)]
    with ExitStack() as mem:
        qT = mem.enter_context(nc.sbuf_tensor("t_qT", [MLA_D, 2, N_MLA, P], F32))
        part = mem.enter_context(nc.sbuf_tensor("t_part", [P, 2, 2], F32))
        at = Attention(core, mem, "t", 5, n_keys, len(pieces))
        ident_in, part_done = core.sem("t_ident_in"), core.sem("t_part_done")
        with nc.Block() as block:
            @block.sync
            def _(sp):
                sp.dma_start(at.ident[:, :], d["ident"]).then_inc(ident_in, 16)

                def body(pair, before):
                    for q in pair:
                        if q.t > 1:
                            sp.wait_ge(at.score_done, q.n * (UNITS * 2) - UNITS * 2)
                            hold(sp, "sp")
                        sp.dma_start(qT[:, q.p, :, :], d["mla_q"].rearrange("(h e) n -> e h n", e=MLA_D)[:, :, bass.ds(q.row, P)])\
                            .then_inc(at.q_in[q.p], 16)
                over_queries(sp, body)

            @block.gpsimd
            def _(pool):
                def body(pair, before):
                    for q in pair:
                        pool.wait_ge(at.out_done, q.n + 1)
                        hold(pool, "pool")
                        pool.dma_start(d["mix_tok"][bass.ds(q.row, P), D_RWKV + D_NA:D], at.out[:, q.p, :, :]
                                       .rearrange("p h e -> p (h e)")).then_inc(at.out_sent[q.p], 16)
                over_queries(pool, body)
                for p in range(2):
                    pool.wait_ge(at.out_sent[p], 8 * NQ)

            @block.scalar
            def _(act):
                def exp(u):
                    act.wait_ge(at.max_done, u.n + 1)
                    hold(act, "act")
                    for lo, hi in pieces:
                        nc.scalar.activation(at.probs[:, u.p, lo:hi], at.ps_s[:, lo:hi], ACT.Exp,
                                             bias=at.stat[:, u.p:u.p + 1]).then_inc(at.exp_done, 1)

                def move(u):
                    at.to_sbuf(act, "act", lambda o, i: nc.scalar.activation(o, i, ACT.Copy), u, 0, groups, tiles)

                def body(pair, before):
                    for u, last in units_of(pair, before):
                        if last:
                            move(last)
                        exp(u)
                move(Unit(over_queries(act, body), UNITS - 1))

            @block.vector
            def _(dve):
                def maximum(u):
                    for i, (lo, hi) in enumerate(halves):
                        dve.wait_ge(at.score_done, u.n * 2 + (i + 1))
                        hold(dve, "dve")
                        nc.vector.tensor_reduce(part[:, u.p, i:i + 1], at.ps_s[:, lo:hi], AX, ALU.max)
                    dve.drain()
                    nc.vector.tensor_reduce(at.stat[:, u.p:u.p + 1], part[:, u.p, :], AX, ALU.max, negate=True)\
                        .then_inc(at.max_done, 1)

                def move(u):
                    for g in range(1, groups):
                        at.to_sbuf(dve, "dve", nc.vector.tensor_copy, u, g, groups, tiles)

                def body(pair, before):
                    for u, last in units_of(pair, before):
                        maximum(u)
                        if last:
                            move(last)
                            if u.h == 0:
                                at.normalise(dve, last.q)
                last = over_queries(dve, body)
                move(Unit(last, UNITS - 1))
                at.normalise(dve, last)

            @block.tensor
            def _(pe):
                def score(u):
                    q = u.q
                    if u.h == 0:
                        pe.wait_ge(at.q_in[q.p], same_parity(q, 16) + 16)
                        hold(pe, "pe")
                    for c, (lo, hi) in enumerate(chunks):
                        if not u.first and c in (0, 2, 4):
                            pe.wait_ge(at.exp_done, u.n * 3 - 2 + c // 2)
                            hold(pe, "pe")
                        mm = nc.tensor.matmul(at.ps_s[:, lo:hi], qT[:, q.p, u.h, :], keys.kT[:, u.h, lo:hi], start=True, stop=True)
                        if c in (2, 4):
                            mm.then_inc(at.score_done, 1)

                def values(u):
                    at.turn_and_multiply(pe, u, u.first, tiles, groups, lambda k: keys.v[:, k, u.h, :])

                def body(pair, before):
                    for u, last in units_of(pair, before):
                        score(u)
                        if last:
                            values(last)
                pe.wait_ge(ident_in, 16)
                values(Unit(over_queries(pe, body), UNITS - 1))


def phase_context_attention(core, l, keys):
    nc, d, hold = core.nc, core.dram, core.hold
    H = UNITS
    with ExitStack() as mem:
        def sb(name, shape):
            return mem.enter_context(nc.sbuf_tensor(name, shape, F32))
        ident = sb("c_ident", [P, P])
        qkT = sb("c_qkT", [HD, 2, H, P])
        qT = sb("c_qT", [MLA_D, H, P])
        v = sb("c_v", [P, H, V_W])
        top = sb("c_top", [P, H])
        shifted = sb("c_shifted", [P, H, P])
        probs = sb("c_probs", [P, H, P])
        probsT = sb("c_probsT", [P, H, P])
        rsum = sb("c_rsum", [P, H])
        out = sb("c_out", [P, 2, H, HD])
        ps_s = mem.enter_context(nc.psum_tensor("c_ps_s", [P, 8, P], F32))
        ps_t = mem.enter_context(nc.psum_tensor("c_ps_t", [P, 8, P], F32))
        ps_o = mem.enter_context(nc.psum_tensor("c_ps_o", [P, H, V_W], F32))
        loaded, ones_done, score_done, shift_done, exp_done, turn_done, moved, value_done, out_done, sent = (
            core.sem(f"c_{n}") for n in ("loaded", "ones_done", "score_done", "shift_done", "exp_done", "turn_done",
                                         "moved", "value_done", "out_done", "sent"))
        with nc.Block() as block:
            @block.sync
            def _(sp):
                sp.wait_ge(ones_done, 1)
                sp.dma_start(ident[:, :], d["ident"]).then_inc(loaded, 16)
                for i in range(2):
                    sp.dma_start(qkT[:, i, :, :], d["feat_attn"][i * D_NA:(i + 1) * D_NA, 0:P]
                                 .rearrange("(h e) n -> e h n", e=HD)).then_inc(loaded, 16)
                sp.dma_start(qT[:, :, :], d["mla_q"].rearrange("(h e) n -> e h n", e=MLA_D)[:, :, 0:P]).then_inc(loaded, 16)
                sp.dma_start(v[:, :, 0:HD], d["vn_tok"][0:P, :].rearrange("p (h e) -> p h e", e=HD)).then_inc(loaded, 16)
                for r, (lo, hi) in enumerate(((D_RWKV, D_RWKV + D_NA), (D_RWKV + D_NA, D))):
                    sp.wait_ge(out_done, (r + 1))
                    sp.dma_start(d["mix_tok"][0:P, lo:hi], out[:, r, :, :].rearrange("p h e -> p (h e)")).then_inc(sent, 16)
                sp.wait_ge(sent, 32)

            @block.gpsimd
            def _(pool):
                nc.gpsimd.memset(v[:, :, :], 1.0).then_inc(ones_done, 1)

            @block.tensor
            def _(pe):
                pe.wait_ge(loaded, 80)
                for r in range(2):
                    if r:
                        pe.wait_ge(shift_done, 1)
                    for h in range(H):
                        a, b = (qkT[:, 0, h, :], qkT[:, 1, h, :]) if r == 0 else (qT[:, h, :], keys.kT[:, h, OWN_COL:OWN_COL + P])
                        mm = nc.tensor.matmul(ps_s[:, h, :], a, b, start=True, stop=True)
                    mm.then_inc(score_done, 1)
                    pe.wait_ge(exp_done, (r + 1))
                    for h in range(H):
                        tr = nc.tensor.transpose(ps_t[:, h, :], probs[:, h, :], ident[:, :])
                    tr.then_inc(turn_done, 1)
                    pe.wait_ge(moved, (r + 1))
                    if r:
                        pe.wait_ge(out_done, 1)
                    for h in range(H):
                        mm = nc.tensor.matmul(ps_o[:, h, :], probsT[:, h, :], v[:, h, :] if r == 0 else keys.v[:, OWN_TILE, h, :],
                                              start=True, stop=True)
                    mm.then_inc(value_done, 1)

            @block.scalar
            def _(act):
                for r in range(2):
                    act.wait_ge(shift_done, (r + 1))
                    nc.scalar.activation(probs[:, :, :], shifted[:, :, :], ACT.Exp).then_inc(exp_done, 1)
                    act.wait_ge(turn_done, (r + 1))
                    nc.scalar.activation(probsT[:, :, :], ps_t[:, 0:H, :], ACT.Copy).then_inc(moved, 1)

            @block.vector
            def _(dve):
                for r in range(2):
                    dve.wait_ge(score_done, (r + 1))
                    nc.vector.tensor_reduce(top[:, :], ps_s[:, 0:H, :], AX, ALU.max)
                    dve.drain()
                    nc.vector.tensor_tensor(shifted[:, :, :], ps_s[:, 0:H, :], top[:, :].unsqueeze(2).broadcast_to([P, H, P]),
                                            ALU.subtract).then_inc(shift_done, 1)
                    dve.wait_ge(value_done, (r + 1))
                    nc.vector.reciprocal(rsum[:, :], ps_o[:, :, HD])
                    dve.drain()
                    nc.vector.tensor_tensor(out[:, r, :, :], ps_o[:, :, 0:HD], rsum[:, :].unsqueeze(2).broadcast_to([P, H, HD]),
                                            ALU.mult).then_inc(out_done, 1)


def phase_output(core, l):
    nc, d, hold = core.nc, core.dram, core.hold
    with ExitStack() as mem:
        def sb(name, shape):
            return mem.enter_context(nc.sbuf_tensor(name, shape, F32))
        w = sb("e_w", [P, KD, D])
        gate_b = sb("e_gate", [P, 2, D])
        ident = sb("e_ident", [P, P])
        mix = sb("e_mix", [P, 2, D])
        gates = sb("e_gates", [P, 2, D])
        th = sb("e_tanh", [P, 2, D])
        mT = sb("e_mT", [P, 2, KD, P])
        x = sb("e_x", [P, 2, D])
        y = sb("e_y", [P, 2, D])
        ps_t = [[mem.enter_context(nc.psum_tensor(f"e_ps_t{p}{i}", [P, 4, P], F32)) for i in range(2)] for p in range(2)]
        ps_y = [[mem.enter_context(nc.psum_tensor(f"e_ps_y{p}{i}", [P, CHUNK], F32)) for i in range(2)] for p in range(2)]
        const_in, w_in = core.sem("e_const_in"), core.sem("e_w_in")
        mix_in = [core.sem(f"e_mix{p}_in") for p in range(2)]
        x_in = [core.sem(f"e_x{p}_in") for p in range(2)]
        y_out = [core.sem(f"e_y{p}_out") for p in range(2)]
        tanh_done, gated, turn_done, mT_done, mm_done, y_done = (
            core.sem(f"e_{n}") for n in ("tanh_done", "gated", "turn_done", "mT_done", "mm_done", "y_done"))
        in_row, out_row = l * TOK, l * TOK + TOK

        with nc.Block() as block:
            @block.sync
            def _(sp):
                sp.dma_start(ident[:, :], d["ident"]).then_inc(const_in, 16)
                for g in range(2):
                    sp.dma_start(gate_b[:, g, :], d["mod_rows"][bass.ds(l * 2 + g, 1), 2 * D:3 * D].broadcast_to([P, D]))\
                        .then_inc(const_in, 16)

                def body(tile):
                    if tile.t > 1:
                        sp.wait_ge(gated, tile.n - 1)
                        hold(sp, "sp")
                    sp.dma_start(mix[:, tile.p, :], d["mix_tok"][bass.ds(tile.row, P), :]).then_inc(mix_in[tile.p], 16)
                    sp.dma_start(gates[:, tile.p, :], d["gate_tok"][bass.ds(tile.row, P), :]).then_inc(mix_in[tile.p], 16)
                    if tile.t == 1:
                        for k in range(KD):
                            sp.dma_start(w[:, k, :], d["w_out"][bass.ds(l, 1), k * P:(k + 1) * P, :]
                                         .rearrange("a p n -> (a p) n")).then_inc(w_in, 16)
                over_tiles(sp, body)

            @block.gpsimd
            def _(pool):
                def store(tile):
                    pool.wait_ge(y_done, tile.n + 1)
                    hold(pool, "pool")
                    pool.dma_start(d["stream"][bass.ds(out_row + tile.row, P), :], y[:, tile.p, :]).then_inc(y_out[tile.p], 16)

                def body(tile):
                    if tile.t > 1:
                        pool.wait_ge(y_done, tile.n - 1)
                        hold(pool, "pool")
                    pool.dma_start(x[:, tile.p, :], d["stream"][bass.ds(in_row + tile.row, P), :]).then_inc(x_in[tile.p], 16)
                    if tile.prev:
                        store(tile.prev)

                store(over_tiles(pool, body))
                for p in range(2):
                    n = 16 * ((NT + 1 - p) // 2)
                    pool.wait_ge(y_out[p], n)
                    hold(pool, "pool")

            @block.scalar
            def _(act):
                def body(tile):
                    act.wait_ge(mix_in[tile.p], of_parity(tile, 32) + 32)
                    hold(act, "act")
                    if tile.t > 1:
                        act.wait_ge(gated, tile.n - 1)
                        hold(act, "act")
                    nc.scalar.activation(th[:, tile.p, :], gates[:, tile.p, :], ACT.Tanh, scale=0.5).then_inc(tanh_done, 1)
                    for i in range(2):
                        act.wait_ge(turn_done, tile.n * 2 + (i + 1))
                        hold(act, "act")
                        if i == 0 and tile.t > 1:
                            act.wait_ge(mm_done, tile.n * 2 - 2)
                            hold(act, "act")
                        nc.scalar.activation(mT[:, tile.p, 4 * i:4 * i + 4, :], ps_t[tile.p][i][:, :, :], ACT.Copy).then_inc(mT_done, 1)
                over_tiles(act, body)

            @block.vector
            def _(dve):
                def gating(tile):
                    dve.wait_ge(mix_in[tile.p], of_parity(tile, 32) + 32)
                    dve.wait_ge(tanh_done, tile.n + 1)
                    hold(dve, "dve")
                    if tile.t > 1:
                        dve.wait_ge(turn_done, tile.n * 2 - 2)
                        hold(dve, "dve")
                    nc.vector.scalar_tensor_tensor(out=gates[:, tile.p, :], in0=th[:, tile.p, :], scalar=1.0,
                                                   in1=gates[:, tile.p, :], op0=ALU.add, op1=ALU.mult)
                    dve.drain()
                    nc.vector.scalar_tensor_tensor(out=th[:, tile.p, :], in0=gates[:, tile.p, :], scalar=0.5,
                                                   in1=mix[:, tile.p, :], op0=ALU.mult, op1=ALU.mult).then_inc(gated, 1)

                def add(tile):
                    g = 1 if tile.t == 0 else 0
                    dve.wait_ge(x_in[tile.p], of_parity(tile, 16) + 16)
                    hold(dve, "dve")
                    if tile.t > 1:
                        dve.wait_ge(y_out[tile.p], of_parity(tile, 16))
                        hold(dve, "dve")
                    for i in range(2):
                        dve.wait_ge(mm_done, tile.n * 2 + (i + 1))
                        hold(dve, "dve")
                        cols = slice(i * CHUNK, (i + 1) * CHUNK)
                        nc.vector.tensor_tensor(y[:, tile.p, cols], ps_y[tile.p][i][:, :], gate_b[:, g, cols], ALU.mult)
                    dve.drain()
                    nc.vector.tensor_tensor(y[:, tile.p, :], y[:, tile.p, :], x[:, tile.p, :], ALU.add).then_inc(y_done, 1)

                def body(tile):
                    gating(tile)
                    if tile.prev:
                        add(tile.prev)
                dve.wait_ge(const_in, 48)
                add(over_tiles(dve, body))

            @block.tensor
            def _(pe):
                def turn(tile):
                    pe.wait_ge(gated, tile.n + 1)
                    hold(pe, "pe")
                    if tile.t > 1:
                        pe.wait_ge(mT_done, tile.n * 2 - 2)
                        hold(pe, "pe")
                    for k in range(KD):
                        tr = nc.tensor.transpose(ps_t[tile.p][k // 4][:, k % 4, :], th[:, tile.p, k * P:(k + 1) * P], ident[:, :])
                        if k % 4 == 3:
                            tr.then_inc(turn_done, 1)

                def products(tile, i):
                    if i == 0:
                        pe.wait_ge(mT_done, tile.n * 2 + 2)
                        if tile.t == 0:
                            pe.wait_ge(w_in, 16 * KD)
                        if tile.t > 1:
                            pe.wait_ge(y_done, tile.n - 1)
                        hold(pe, "pe")
                    for k in range(KD):
                        mm = nc.tensor.matmul(ps_y[tile.p][i][:, :], mT[:, tile.p, k, :], w[:, k, i * CHUNK:(i + 1) * CHUNK],
                                              start=(k == 0), stop=(k == KD - 1))
                    mm.then_inc(mm_done, 1)

                def body(tile):
                    if tile.prev:
                        products(tile.prev, 0)
                    turn(tile)
                    if tile.prev:
                        products(tile.prev, 1)
                pe.wait_ge(const_in, 48)
                last = over_tiles(pe, body)
                for i in range(2):
                    products(last, i)


def build(nc, d):
    core = Core(nc, d)
    with core.phase():
        phase_modulation(core)
    with nc.Fori(0, DEPTH) as l:
        for phase in (phase_projection, phase_scans, phase_scan_output, phase_neighbourhood):
            with core.phase():
                phase(core, l)
        with ExitStack() as mem:
            keys = LatentKeys(core, mem)
            for phase in (phase_latent_keys, phase_context_attention, phase_latent_attention):
                with core.phase():
                    phase(core, l, keys)
        with core.phase():
            phase_output(core, l)


def _constants():
    import numpy as _np
    t = _np.arange(LAT)
    inv = _np.power(10000.0, -_np.arange(ROPE // 4, dtype=_np.float32) / (ROPE // 4)).astype(_np.float32)
    ang = _np.concatenate([(t // GRID).astype(_np.float32)[:, None] * inv, (t % GRID).astype(_np.float32)[:, None] * inv], -1)
    rope = _np.concatenate([_np.cos(ang), _np.sin(ang)], -1)
    still = _np.concatenate([_np.ones((CTX, ROPE // 2)), _np.zeros((CTX, ROPE // 2))], -1)
    q = _np.arange(P) % GRID
    start = _np.clip(q - NA_COLS // 2, 0, GRID - NA_COLS)[:, None]
    c = _np.arange(GRID)[None, :]
    i, j = _np.arange(C)[:, None], _np.arange(C)[None, :]
    later = [i > j, i < j]
    levels = [[(i // (2 * b) == j // (2 * b)) & (i // b != j // b) & m for m in later] for b in (1, 2, 4, 8, 16, 32)]
    chunk = [[-1.0 * m.T for m in later], [m.T | (i == j) for m in later], [i == j] * 2]
    m = [_np.broadcast_to(_np.stack(x, 1)[None], (2, C, 2, C)) for x in chunk]
    minus = [[-1.0 * y for y in x] for x in levels]
    pair = [_np.stack([_np.kron(_np.eye(2), y) for y in x], 1) for x in ([m.T for m in minus[0]], [i == j] * 2, *minus)]
    return {
        "rope": _np.concatenate([still, rope], 0).astype(_np.float32),
        "col_mask": _np.where((c >= start) & (c < start + NA_COLS), 0.0, NEG).astype(_np.float32),
        "flip": (_np.arange(GRID)[:, None] == GRID - 1 - q[None, :]).astype(_np.float32),
        "ident": _np.eye(P, dtype=_np.float32),
        "masks": _np.repeat(_np.stack(m, 0).transpose(1, 2, 0, 3, 4), 2, 3).reshape(P, 3, 4, C).astype(_np.float32),
        "wide_masks": _np.stack(pair, 1).astype(_np.float32),
        "head_ones": _np.kron(_np.eye(2), _np.ones((HD, HD))).astype(_np.float32),
        "head_sel": _np.kron(_np.eye(2), _np.ones((HD, 1))).astype(_np.float32),
        "half_sel": _np.stack([_np.eye(P, HD), _np.eye(P, HD, -HD)], 1).astype(_np.float32),
        "reset": _np.broadcast_to((_np.arange(4 * P) % C > 0).astype(_np.float32), (P, 4 * P)),
    }


def _features(a):
    import numpy as _np
    rows = [a["rwkv_conv"].reshape(DEPTH, 18, P), a["rwkv_k_k"].reshape(DEPTH, 2, P), a["rwkv_k_a"].reshape(DEPTH, 2, P),
            a["rwkv_r_k"].reshape(DEPTH, 2, P), a["rwkv_w0"].reshape(DEPTH, 4, P), a["rwkv_a0"].reshape(DEPTH, 4, P)]
    return _np.concatenate(rows, 1).transpose(0, 2, 1).reshape(DEPTH * P, N_FEAT_PAR)


def _arrays(inputs):
    import numpy as _np
    a = {k: _np.asarray(v) for k, v in inputs.items()}
    cat = _np.concatenate
    out = {
        "x": cat([a["x_prompt"][0], a["x_sample"][0]], 0),
        "cond": _np.stack([a["c"][0], a["c_ctx"]], -1).reshape(KD, P, 2).transpose(1, 0, 2),
        "w_mod": a["w_mod"],
        "b_mod": _np.broadcast_to(a["b_mod"].reshape(1, -1), (2, DEPTH * 3 * D)),
        "norm_w": a["norm_w"],
        "w_in": a["w_in"],
        "norm_rows": cat([a["na_q_norm"], a["na_k_norm"], a["mla_cq_norm"], a["mla_ckv_norm"]], -1),
        "w_out": a["w_out"],
        "rwkv_par": _features(a),
        "w_up": a["rwkv_w_up"].transpose(0, 2, 1, 3).reshape(DEPTH * LORA, 2, D_RWKV),
        "a_up": a["rwkv_a_up"].transpose(0, 2, 1, 3).reshape(DEPTH * LORA, 2, D_RWKV),
        "state0": a["state_rwkv"][0].reshape(DEPTH, 2, 2, 2, HD, HD).transpose(0, 1, 5, 3, 2, 4).reshape(DEPTH * 2 * HD, 2, 2, HD),
        "rwkv_ln": _np.stack([a["rwkv_ln_w"], a["rwkv_ln_b"]], 1),
        "rpb_pad": _np.pad(a["na_rpb"].reshape(-1, 2 * NA_COLS - 1), ((0, 0), (GRID - NA_COLS, P - GRID - NA_COLS + 1))),
        "na_kT": a["cache_na_k"][0].reshape(DEPTH, PAST, D_NA).transpose(0, 2, 1).reshape(DEPTH * D_NA, PAST),
        "na_v": a["cache_na_v"][0].reshape(DEPTH * PAST, D_NA),
        "past_ckvT": a["cache_mla_ckv"][0].transpose(0, 2, 1),
        "past_krope": a["cache_mla_krope"][0].reshape(DEPTH * PAST, ROPE),
        "w_uk": a["mla_w_uk"],
        "w_uv": a["mla_w_uv"],
        "w_uq": a["mla_w_uq"],
        "mla_q_norm": a["mla_q_norm"],
        "mla_k_norm": a["mla_k_norm"],
        **_constants(),
    }
    return {k: _np.ascontiguousarray(v) for k, v in out.items()}


_SCRATCH = {
    "mod_rows": (DEPTH * 2, 3 * D),
    "feat_rwkv": (len(TURN_RWKV) * P, FEAT_W),
    "feat_attn": (len(TURN_ATTN) * P, TOK),
    "gate_tok": (TOK, D),
    "vn_tok": (TOK, D_NA),
    "krope_tok": (TOK, ROPE),
    "mla_q": (N_MLA * MLA_D, TOK),
    "mix_tok": (TOK, D),
    "scan_tok": (2 * TOK, D_RWKV),
    "bonus_tok": (2 * TOK, D_RWKV),
}
_OUTS = {
    "stream": ((DEPTH + 1) * TOK, D),
    "new_k": (DEPTH * CTX, D_NA),
    "new_v": (DEPTH * CTX, D_NA),
    "new_ckv": (DEPTH * CTX, KV_RANK),
    "new_krope": (DEPTH * CTX, ROPE),
    "new_state": (DEPTH * 2 * HD, 2, 2, HD),
}


def kernel(**inputs):
    import numpy as _np
    import concourse.bacc as _bacc
    from concourse.bass_utils import run_bass_kernel_spmd as _run

    nc = _bacc.Bacc("TRN2", target_bir_lowering=False, num_devices=1)
    arrays = _arrays(inputs)
    dram = {k: nc.dram_tensor(k, v.shape, F32, kind="ExternalInput").ap() for k, v in arrays.items()}
    for k, shape in _OUTS.items():
        dram[k] = nc.dram_tensor(k, shape, F32, kind="ExternalOutput").ap()
    for k, shape in _SCRATCH.items():
        dram[k] = nc.dram_tensor(k, shape, F32, kind="Internal").ap()
    build(nc, dram)
    r = _run(nc, [arrays], core_ids=[0]).results[0]
    y = r["stream"][DEPTH * TOK:]
    cache = lambda name, *shape: r[name].reshape(DEPTH, 1, CTX, *shape).transpose(1, 0, *range(2, 3 + len(shape)))
    state = r["new_state"].reshape(DEPTH, 2, HD, 2, 2, HD).transpose(0, 1, 4, 3, 5, 2).reshape(DEPTH, 2, N_RWKV, HD, HD)
    return (y[None, :CTX], y[None, CTX:], _np.ascontiguousarray(state)[None],
            cache("new_k", N_NA, HD), cache("new_v", N_NA, HD), cache("new_ckv", KV_RANK), cache("new_krope", ROPE))
```
